# Optimizing a Trainium2 kernel written in Bass

```python
import jax, jax.numpy as jnp
from jax import lax
import numpy as np

D_MODEL = 1024
BATCH = 1
SEQ = 256
DEPTH = 2

N_MEM = 256
POOL_WINDOWS = (2, 4, 8, 16)
N_POOL_GROUPS = 4
POOL_WIDTH = D_MODEL // 2
POOL_GROUP = POOL_WIDTH // N_POOL_GROUPS
CONV_WIDTH = D_MODEL // 2
CONV_K = 3
N_XHEADS = 4
XHEAD_DIM = D_MODEL // N_XHEADS
D_FF = 2816
N_EXPERTS = 8
TOP_K = 2
D_FF_EXPERT = 3584
EPS = 1e-6
N_DENSE = (DEPTH + 1) // 2
N_MOE = DEPTH // 2
IN_WIDTH = POOL_WIDTH + 3 * CONV_WIDTH + 2 * D_MODEL

kernel_name = "hybrid_pool_shortconv_xattn_moe"

def rmsnorm(x, g):
    xf = x.astype(jnp.float32)
    y = xf * lax.rsqrt(jnp.mean(xf * xf, axis=-1, keepdims=True) + EPS)
    return (y * g.astype(jnp.float32)).astype(x.dtype)

def pool_mixer(u, w_group, scale):
    s = u.shape[1]
    uf = u.astype(jnp.float32)
    pos1 = jnp.arange(1, s + 1, dtype=jnp.float32)[None, :, None]
    outs = []
    for g, w in enumerate(POOL_WINDOWS):
        ug = uf[..., g * POOL_GROUP:(g + 1) * POOL_GROUP]
        cs = jnp.cumsum(ug, axis=1)
        lag = jnp.pad(cs, ((0, 0), (w, 0), (0, 0)))[:, :s]
        mean = (cs - lag) / jnp.minimum(pos1, float(w))
        outs.append(mean - ug)
    p = jnp.stack(outs, axis=2).astype(u.dtype)
    y = jnp.einsum('bsgc,gcd->bsgd', p, w_group)
    return y.reshape(u.shape) * scale

def short_conv(z, conv_w):
    s = z.shape[1]
    zp = jnp.pad(z, ((0, 0), (CONV_K - 1, 0), (0, 0)))
    y = conv_w[0] * zp[:, 0:s]
    for k in range(1, CONV_K):
        y = y + conv_w[k] * zp[:, k:k + s]
    return y

def cross_attention(h, mem_n, wq, wk, wv, wo):
    b, s, _ = h.shape
    m = mem_n.shape[1]
    q = (h @ wq).reshape(b, s, N_XHEADS, XHEAD_DIM)
    k = (mem_n @ wk).reshape(b, m, N_XHEADS, XHEAD_DIM)
    v = (mem_n @ wv).reshape(b, m, N_XHEADS, XHEAD_DIM)
    sc = jnp.einsum('bshd,bmhd->bhsm', q, k).astype(jnp.float32) * (XHEAD_DIM ** -0.5)
    p = jax.nn.softmax(sc, axis=-1).astype(v.dtype)
    o = jnp.einsum('bhsm,bmhd->bshd', p, v).reshape(b, s, D_MODEL)
    return o @ wo

def swiglu(h, wg, wu, wd):
    return (jax.nn.silu(h @ wg) * (h @ wu)) @ wd

def moe_ffn(h, w_router, wg, wu, wd):
    b, s, d = h.shape
    hf = h.reshape(b * s, d)
    logits = (hf @ w_router).astype(jnp.float32)
    topv, topi = lax.top_k(logits, TOP_K)
    wts = jax.nn.softmax(topv, axis=-1)
    gate = jnp.sum(jax.nn.one_hot(topi, N_EXPERTS, dtype=jnp.float32) * wts[..., None], axis=1)
    out = jnp.zeros_like(hf)
    for e in range(N_EXPERTS):
        out = out + gate[:, e:e + 1].astype(hf.dtype) * swiglu(hf, wg[e], wu[e], wd[e])
    return out.reshape(b, s, d)

def setup_inputs(seed: int = 0) -> dict:
    key = jax.random.key(seed)
    ks = jax.random.split(key, 32)
    f32 = jnp.float32

    def nrm(k, shape, fan_in):
        return jax.random.normal(k, shape, f32) * (fan_in ** -0.5)

    def gain(k, shape):
        return 1.0 + 0.05 * jax.random.normal(k, shape, f32)

    return {
        "x": jax.random.normal(ks[0], (BATCH, SEQ, D_MODEL), f32),
        "mem": jax.random.normal(ks[1], (BATCH, N_MEM, D_MODEL), f32),
        "g_mix": gain(ks[2], (DEPTH, D_MODEL)),
        "w_in": nrm(ks[3], (DEPTH, D_MODEL, IN_WIDTH), D_MODEL),
        "w_pool_group": nrm(ks[4], (DEPTH, N_POOL_GROUPS, POOL_GROUP, POOL_GROUP), POOL_GROUP),
        "pool_scale": gain(ks[5], (DEPTH, POOL_WIDTH)),
        "w_pool_out": nrm(ks[6], (DEPTH, POOL_WIDTH, D_MODEL), POOL_WIDTH),
        "conv_w": nrm(ks[7], (DEPTH, CONV_K, CONV_WIDTH), CONV_K),
        "w_conv_out": nrm(ks[8], (DEPTH, CONV_WIDTH, D_MODEL), CONV_WIDTH),
        "w_mix_out": nrm(ks[9], (DEPTH, D_MODEL, D_MODEL), D_MODEL),
        "g_xattn": gain(ks[10], (DEPTH, D_MODEL)),
        "g_mem": gain(ks[11], (DEPTH, D_MODEL)),
        "w_xq": nrm(ks[12], (DEPTH, D_MODEL, D_MODEL), D_MODEL),
        "w_xk": nrm(ks[13], (DEPTH, D_MODEL, D_MODEL), D_MODEL),
        "w_xv": nrm(ks[14], (DEPTH, D_MODEL, D_MODEL), D_MODEL),
        "w_xo": nrm(ks[15], (DEPTH, D_MODEL, D_MODEL), D_MODEL),
        "g_ffn": gain(ks[16], (DEPTH, D_MODEL)),
        "w_ff_gate": nrm(ks[17], (N_DENSE, D_MODEL, D_FF), D_MODEL),
        "w_ff_up": nrm(ks[18], (N_DENSE, D_MODEL, D_FF), D_MODEL),
        "w_ff_down": nrm(ks[19], (N_DENSE, D_FF, D_MODEL), D_FF),
        "w_router": nrm(ks[20], (N_MOE, D_MODEL, N_EXPERTS), D_MODEL),
        "w_e_gate": nrm(ks[21], (N_MOE, N_EXPERTS, D_MODEL, D_FF_EXPERT), D_MODEL),
        "w_e_up": nrm(ks[22], (N_MOE, N_EXPERTS, D_MODEL, D_FF_EXPERT), D_MODEL),
        "w_e_down": nrm(ks[23], (N_MOE, N_EXPERTS, D_FF_EXPERT, D_MODEL), D_FF_EXPERT),
        "g_final": gain(ks[24], (D_MODEL,)),
    }

def reference(x, mem, g_mix, w_in, w_pool_group, pool_scale, w_pool_out, conv_w, w_conv_out, w_mix_out,
              g_xattn, g_mem, w_xq, w_xk, w_xv, w_xo, g_ffn, w_ff_gate, w_ff_up, w_ff_down,
              w_router, w_e_gate, w_e_up, w_e_down, g_final):
    o_c = POOL_WIDTH
    o_b = o_c + CONV_WIDTH
    o_u = o_b + CONV_WIDTH
    o_g = o_u + CONV_WIDTH
    for l in range(DEPTH):
        h = rmsnorm(x, g_mix[l])
        z = h @ w_in[l]
        u_pool = z[..., :o_c]
        c_gate = z[..., o_c:o_b]
        b_gate = z[..., o_b:o_u]
        u_conv = z[..., o_u:o_g]
        gates = jax.nn.sigmoid(z[..., o_g:].astype(jnp.float32)).astype(x.dtype)
        y_pool = pool_mixer(u_pool, w_pool_group[l], pool_scale[l]) @ w_pool_out[l]
        y_conv = (b_gate * short_conv(c_gate * u_conv, conv_w[l])) @ w_conv_out[l]
        merged = gates[..., :D_MODEL] * y_pool + gates[..., D_MODEL:] * y_conv
        x = x + merged @ w_mix_out[l]
        h = rmsnorm(x, g_xattn[l])
        mem_n = rmsnorm(mem, g_mem[l])
        x = x + cross_attention(h, mem_n, w_xq[l], w_xk[l], w_xv[l], w_xo[l])
        h = rmsnorm(x, g_ffn[l])
        if l % 2 == 0:
            i = l // 2
            x = x + swiglu(h, w_ff_gate[i], w_ff_up[i], w_ff_down[i])
        else:
            i = l // 2
            x = x + moe_ffn(h, w_router[i], w_e_gate[i], w_e_up[i], w_e_down[i])
    return rmsnorm(x, g_final)


_drawn_inputs = setup_inputs


def setup_inputs(seed=0):
    import zlib

    import numpy as np

    out = dict(_drawn_inputs(seed))
    spreads = {}
    factors = {'g_xattn': 3.273, 'g_mem': 2.887}
    for name, (base, spread) in spreads.items():
        noise = np.random.default_rng([zlib.crc32(name.encode()), seed]).standard_normal(out[name].shape)
        drawn = base * np.exp(spread * noise) if base else spread * noise
        out[name] = __import__('jax').numpy.asarray(drawn.astype(out[name].dtype))
    for name, factor in factors.items():
        out[name] = (out[name] * factor).astype(out[name].dtype)
    return out
```

```python
import concourse.bass as bass
from concourse import mybir

F32 = mybir.dt.float32
F32R = mybir.dt.float32r
I32 = mybir.dt.int32
ALU = mybir.AluOpType
ACT = mybir.ActivationFunctionType
AX_X = mybir.AxisListType.X

P = 128
EPS = 1e-6
UNIT = 2048
RAW = 6
SPL = 3
BIG = 3.0e38


def trunk(nc, a, out):
    SEQ, D = a["x"].shape[1:]
    DEPTH = a["w_in"].shape[0]
    NT, KD = SEQ // P, D // P
    HALF = D // 2
    NG = HALF // P
    DFF = a["w_ff_gate"].shape[2]
    NE, DFE = a["w_e_gate"].shape[1], a["w_e_gate"].shape[3]
    NH = 4
    HD = D // NH
    C = 512
    NJ = DFE // C
    BODY = 6 * NJ
    WINDOWS = (2, 4, 8, 16)
    PAD = max(WINDOWS)
    CK = a["conv_w"].shape[1]
    FH = DFF // 2
    FT = FH // P
    FCH = [(c, min(C, FH - c)) for c in range(0, FH, C)]
    assert NT == 2 and KD == 8 and NG == 4 and DEPTH == 2 and FH % P == 0 and BODY % RAW == 0

    units = []

    def add_units(w, kts, col, cols):
        per = UNIT // cols if cols == C else 4
        for k in range(0, kts, per):
            units.append((w, k, min(per, kts - k), col, cols))

    def add_square(w, chunks=(0, 1)):
        for c in chunks:
            add_units(w, KD, c * C, C)

    add_square(a["w_xk"][0])
    add_square(a["w_xv"][0], (0,))
    z_start, q_start = [], []
    for l in range(DEPTH):
        z_start.append(len(units))
        for c in range(a["w_in"].shape[2] // C):
            add_units(a["w_in"][l], KD, c * C, C)
        for w in (a["w_pool_out"][l], a["w_conv_out"][l]):
            for c in range(2):
                add_units(w, NG, c * C, C)
        add_square(a["w_mix_out"][l])
        add_square(a["w_xv"][l], (1,))
        q_start.append(len(units))
        add_square(a["w_xq"][l])
        add_square(a["w_xo"][l])
        if l == 0:
            add_square(a["w_xk"][1])
            for f in range(2):
                for c, n in FCH:
                    add_units(a["w_ff_gate"][0], KD, f * FH + c, n)
                    add_units(a["w_ff_up"][0], KD, f * FH + c, n)
                for c in range(2):
                    add_units(a["w_ff_down"][0][f * FH:(f + 1) * FH, :], FT, c * C, C)
            add_square(a["w_xv"][1], (0,))
    U0 = len(units)

    G_MIX, G_XATTN, G_MEM, G_FFN = (i * DEPTH * KD for i in range(4))
    R_CONV = 4 * DEPTH * KD
    R_SCALE = R_CONV + DEPTH * CK * NG
    ROWS = R_SCALE + DEPTH * NG

    base = (nc.sbuf_base + 63) // 64 * 64
    at = {"top": base}

    def place(name, shape, dt, where=None):
        size = 4
        for s in shape[1:]:
            size *= s
        if where is None:
            where = at["top"]
            at["top"] += (size + 63) // 64 * 64
        return nc.alloc_sbuf_tensor_at(name, shape, dt, offset=where)

    raw = [place(f"raw{i}", [P, UNIT], F32) for i in range(RAW)]
    whi = [place(f"whi{i}", [P, UNIT], F32R) for i in range(SPL)]
    wlo = [place(f"wlo{i}", [P, UNIT], F32R) for i in range(SPL)]
    x = place("x_res", [P, NT, D], F32)
    Ah = place("a_hi", [P, KD, SEQ], F32R)
    Al = place("a_lo", [P, KD, SEQ], F32R)
    Bh = place("b_hi", [P, KD, SEQ], F32R)
    Bl = place("b_lo", [P, KD, SEQ], F32R)
    Mh = place("mem_hi", [P, KD, SEQ], F32R)
    Ml = place("mem_lo", [P, KD, SEQ], F32R)
    kT = place("kT", [P, KD, SEQ], F32)
    vv = place("v_tok", [P, NT, D], F32)
    moe_top = at["top"]
    gT = place("gatesT", [P, 2 * KD, SEQ], F32)
    sc = at["top"]
    at["top"] += 32768
    ident = place("ident", [P, P], F32)
    cT = place("consts_t", [P, ROWS], F32)
    inv = place("inv_count", [P, NG, PAD], F32)
    wpg = place("w_group", [P, NG, P], F32)
    wrt = place("w_rout", [P, KD, NE], F32)
    NORMS = 9
    ss = place("sumsq", [P, NORMS, 2, NT], F32)
    sst = place("sumsq_t", [P, NORMS, 2, NT], F32)
    rstd = place("rstd", [P, NORMS, NT], F32)
    mhalf = place("minus_half", [P, NT], F32)
    mx = place("max_s", [P, DEPTH, NH, NT], F32)
    nmx = place("neg_max", [P, DEPTH, NH, NT], F32)
    sm = place("sum_s", [P, DEPTH, NH, NT], F32)
    rs = place("rsum_s", [P, DEPTH, NH, NT], F32)
    assert at["top"] <= nc.sbuf_usable_end, (at["top"], nc.sbuf_usable_end)
    arena_size = at["top"] - nc.sbuf_base

    xn = place("x_norm", [P, NT, D], F32, sc)
    xm = place("mem_norm", [P, NT, D], F32, sc + 24576)
    rows = place("const_rows", [P, P], F32, sc + 8192)
    cg = place("c_gateT", [P, NG, SEQ], F32, sc)
    bg = place("b_gateT", [P, NG, SEQ], F32, sc + 4096)
    up = place("u_pool_pad", [P, NG, PAD + SEQ], F32, sc + 8192)
    s1 = place("win_sum1", [P, NG, PAD + SEQ], F32, sc + 12544)
    s2 = place("win_sum2", [P, NG, PAD + SEQ], F32, sc + 16896)
    pp = place("pooledT", [P, NG, SEQ], F32, sc + 21248)
    zc = place("conv_in_pad", [P, NG, CK - 1 + SEQ], F32, sc + 25344)
    qT = place("qT", [P, KD, SEQ], F32, sc)
    pr = place("probs", [P, NH, NT, SEQ], F32, sc + 8192)
    pT = place("probsT", [P, NH, NT, SEQ], F32, sc + 16384)
    Fh = place("ff_hi", [P, FT, SEQ], F32R, sc)
    Fl = place("ff_lo", [P, FT, SEQ], F32R, sc + FT * SEQ * 4)
    st2 = [place(f"ff_tmp{i}", [P, 4, SEQ], F32, sc + 22528 + 4096 * i) for i in range(2)]
    hg = place("h_tok", [P, NT, D], F32, sc + 8192)
    hTf = place("hT_full", [P, KD, SEQ], F32, sc + 16384)
    gbc = place("g_rows", [P, D], F32, sc + 24576)
    m0 = moe_top

    def moe(name, shape, dt):
        t = place(name, shape, dt, m0 + moe.off)
        n = 4
        for s in shape[1:]:
            n *= s
        moe.off += (n + 63) // 64 * 64
        assert moe.off <= 16384
        return t
    moe.off = 0
    S = moe("sel_tok", [P, NT, P], F32R)
    ST = moe("sel_slot", [P, SEQ], F32R)
    gc = moe("gate_slot", [P, 1], F32)
    iota = moe("iota_slots", [P, P], F32)
    tri = moe("strict_upper", [P, P], F32)
    ones = moe("ones", [P, P], F32)
    silu_t = moe("silu_tmp", [P, C], F32)
    act_t = moe("act_tok", [P, C], F32)
    rev = moe("rev_index", [P, NT, NE], F32)
    lg = moe("logits", [P, NT, NE], F32)
    rt = [moe(f"route{i}", [P, NT, NE], F32) for i in range(6)]
    rc = [moe(f"route_c{i}", [P, NT], F32) for i in range(8)]
    posm = moe("rank", [P, NT, 2 * NE + 1], F32)
    gate2 = moe("gate", [P, NT, 2 * NE], F32)
    cnt = moe("count", [P, 2], F32)
    nvis = moe("n_visits", [P, 2], I32)
    aTh = [Mh[:, 2 * i:2 * i + 2, :].rearrange("p a b -> p (a b)").rearrange("p (f c) -> p f c", c=P) for i in range(2)]
    aTl = [Ml[:, 2 * i:2 * i + 2, :].rearrange("p a b -> p (a b)").rearrange("p (f c) -> p f c", c=P) for i in range(2)]
    yh = Mh[:, 4:8, :].rearrange("p a b -> p (a b)")
    yl = Ml[:, 4:8, :].rearrange("p a b -> p (a b)")
    hth = Bh[:, :, :].rearrange("p a b -> p (a b)").rearrange("p (t d) -> p t d", t=NT)
    htl = Bl[:, :, :].rearrange("p a b -> p (a b)").rearrange("p (t d) -> p t d", t=NT)
    heh = Ah[:, 0:4, :].rearrange("p a b -> p (a b)").rearrange("p (k c) -> p k c", c=P)
    hel = Al[:, 0:4, :].rearrange("p a b -> p (a b)").rearrange("p (k c) -> p k c", c=P)

    names = """const_loaded mem_loaded x_loaded wpg_loaded wrt_loaded gbc_loaded setup_done consts_done consts_used
        hi_ready lo_ready unit_used sumsq_ready rstd_ready xn_ready tp_done hi_evac h_ready pads_ready u_ready b_ready
        pooled_ready group_done yp_ready conv_ready yc_ready gate_ready merged_f merged_ready x_ready kv_ready q_ready
        scores_done max_ready exp_done probs_ready pT_ready o_done o_ready silu_done ff_act ff_ready mixer_read
        attn_done act_chain dve_chain pool_chain
        hT_ready hg_ready hgh_ready htok_ready logits_done sel_ready rank_done exp2_done visits_ready zero_done
        t_done g_done sc_done ts_done silu_ready acthi_ready hehi_ready yhi_ready act_ready actT_ready he_ready y_ready
        xadd_done st_ready s_ready tail_y tail_yl tail_sc tail_x tail_ss tail_r tail_o gfin_loaded stored""".split()

    import contextlib
    with contextlib.ExitStack() as ctx:
        ctx.enter_context(nc.sbuf_tensor("arena", [P, arena_size // 4], F32))
        ps = ctx.enter_context(nc.psum_tensor("ps", [P, 8, 512], F32))
        s = {n: ctx.enter_context(nc.semaphore(n)) for n in names}
        raw_loaded = [ctx.enter_context(nc.semaphore(f"raw_loaded{i}")) for i in range(RAW)]
        pair_free = [ctx.enter_context(nc.semaphore(f"pair_free{i}")) for i in range(3)]
        tp_free = [ctx.enter_context(nc.semaphore(f"tp_free{i}")) for i in range(2)]

        def pair(c):
            b = 2 * (c % 3)
            return ps[:, b:b + 2, :].rearrange("p a b -> p (a b)")

        def tiles_of(c, n=4):
            return pair(c)[:, 0:n * SEQ].rearrange("p (d t) -> p d t", t=SEQ)

        def bank(b):
            return ps[:, b, :]

        class At:
            def __init__(self):
                self.u = self.c = self.q = self.n = self.h = 0

        def unit_view(t, u):
            _, _, nk, _, nn = units[u]
            return t[:, 0:nk * nn].rearrange("p (k n) -> p k n", k=nk)

        def cols(ap, c):
            return ap[:, :, c * C:(c + 1) * C]

        def expert_unit(i):
            if i < 4:
                return 0, ("gate", "gate", "up", "up")[i], i % 2
            j, r = divmod(i - 4, 6)
            j += 1
            if j == NJ:
                return NJ - 1, "down", r
            if r < 4:
                return j, ("gate", "gate", "up", "up")[r], r % 2
            return j - 1, "down", r - 4

        def gu_start(j):
            return 0 if j == 0 else 4 + 6 * (j - 1)

        def u_free(c):
            return c // 3 + 1

        with nc.Block() as block:

            @block.sync
            def _(sp):
                def load_unit(u):
                    w, k, nk, col, nn = units[u]
                    if u >= RAW:
                        sp.wait_ge(s["lo_ready"], u - RAW + 1)
                    sp.dma_start(unit_view(raw[u % RAW], u),
                                 w[k * P:(k + nk) * P, col:col + nn].rearrange("(k p) n -> p k n", p=P)
                                 ).then_inc(raw_loaded[u % RAW], 16)

                mem_rows = a["mem"][0].rearrange("(t p) d -> p t d", p=P)
                sp.dma_start(xm[:], mem_rows).then_inc(s["mem_loaded"], 16)
                sp.dma_start(x[:], a["x"][0].rearrange("(t p) d -> p t d", p=P)).then_inc(s["x_loaded"], 16)
                for u in range(4):
                    load_unit(u)
                sp.dma_start(wpg[:], a["w_pool_group"][0].rearrange("g c d -> c g d")).then_inc(s["wpg_loaded"], 16)
                sp.dma_start(wrt[:], a["w_router"][0].rearrange("(k p) e -> p k e", p=P)).then_inc(s["wrt_loaded"], 16)
                for u in range(4, U0):
                    if u == q_start[0] + 4:
                        sp.wait_ge(s["merged_ready"], 2)
                        sp.dma_start(xm[:], mem_rows).then_inc(s["mem_loaded"], 16)
                        sp.wait_ge(s["group_done"], 1)
                        sp.dma_start(wpg[:], a["w_pool_group"][1].rearrange("g c d -> c g d")).then_inc(s["wpg_loaded"], 16)
                    load_unit(u)
                sp.wait_ge(s["merged_ready"], 2 * DEPTH)
                sp.dma_start(gbc[:], a["g_ffn"][1:2, :].broadcast_to([P, D])).then_inc(s["gbc_loaded"], 16)

                def load_expert_unit(i, e, v):
                    u = U0 + i
                    t = raw[u % RAW]
                    j, w, part = expert_unit(i)
                    if w == "down":
                        src = a["w_e_down"][0][bass.ds(e, 1), (j * 4 + part * 2) * P:(j * 4 + part * 2 + 2) * P, :]
                        dst = t[:, :].rearrange("p (k n) -> p k n", k=2)
                    else:
                        src = a["w_e_" + w][0][bass.ds(e, 1), part * C:(part + 1) * C, j * C:(j + 1) * C]
                        dst = t[:, :].rearrange("p (k n) -> p k n", k=4)
                    sp.wait_ge(s["lo_ready"], v * BODY + (u - RAW + 1))
                    sp.dma_start(dst, src.rearrange("e (k p) n -> p (e k) n", p=P)).then_inc(raw_loaded[u % RAW], 16)

                with sp.Fori(0, NE) as e:
                    for i in range(BODY):
                        load_expert_unit(i, e, e)
                sp.wait_ge(s["visits_ready"], 1)
                visits = sp.value_load(nvis[0:1, 0:1], min_val=NE, max_val=2 * NE)
                with sp.If(visits > NE):
                    with sp.Fori(0, NE) as e:
                        for i in range(BODY):
                            load_expert_unit(i, e, e + NE)
                sp.dma_start(gbc[:], a["g_final"].rearrange("(a d) -> a d", a=1).broadcast_to([P, D])
                             ).then_inc(s["gfin_loaded"], 16)

            @block.gpsimd
            def _(pool):
                chain = [0]

                def link(ins):
                    chain[0] += 1
                    ins.then_inc(s["pool_chain"], 1)
                    pool.wait_ge(s["pool_chain"], chain[0])

                link(pool.memset(ident[:], 0.0))
                link(pool.affine_select(out=ident[:], in_=ident[:], compare_op=ALU.not_equal, fill=1.0, base=0,
                                        pattern=[[-1, P]], channel_multiplier=1))
                link(pool.memset(mhalf[:], -0.5))
                link(pool.iota(inv[:, :, :], pattern=[[0, NG], [1, PAD]], base=1, channel_multiplier=0,
                               allow_small_or_imprecise_dtypes=True))
                for g, w in enumerate(WINDOWS):
                    link(pool.tensor_scalar(inv[:, g, :], inv[:, g, :], float(w), None, ALU.min))
                pool.memset(rows[ROWS // 32 * 32:, :], 0.0).then_inc(s["setup_done"], 1)

                def root(n, parts):
                    pool.wait_ge(s["sumsq_ready"], parts)
                    link(pool.tensor_tensor(sst[:, n, 0, :], ss[:, n, 0, :], ss[:, n, 1, :], ALU.add))
                    link(pool.tensor_scalar(sst[:, n, 1, :], sst[:, n, 0, :], 1.0 / D, EPS, ALU.mult, ALU.add))
                    pool.tensor_tensor(rstd[:, n, :], sst[:, n, 1, :], mhalf[:], ALU.pow).then_inc(s["rstd_ready"], 1)

                def pads(u_first):
                    pool.wait_ge(s["unit_used"], u_first + 1)
                    pool.memset(up[:, :, 0:PAD], 0.0)
                    pool.memset(zc[:, :, 0:CK - 1], 0.0).then_inc(s["pads_ready"], 1)

                root(0, 4)
                root(1, 8)
                pads(z_start[0])
                for n in range(2, 6):
                    root(n, 4 * n + 4)
                pads(z_start[1])
                root(6, 28)
                pool.wait_ge(s["merged_ready"], 2 * DEPTH)
                link(pool.iota(iota[:, :], pattern=[[1, P]], base=0, channel_multiplier=0,
                               allow_small_or_imprecise_dtypes=True))
                link(pool.iota(rev[:, :, :], pattern=[[0, NT], [-1, NE]], base=NE, channel_multiplier=0,
                               allow_small_or_imprecise_dtypes=True))
                link(pool.memset(ones[:], 1.0))
                link(pool.affine_select(out=tri[:], in_=ones[:], compare_op=ALU.is_gt, fill=0.0, base=0,
                                        pattern=[[1, P]], channel_multiplier=-1))
                pool.memset(posm[:, :, 2 * NE:2 * NE + 1], -1000.0).then_inc(s["setup_done"], 1)
                root(7, 32)

            @block.scalar
            def _(act):
                p = At()

                def copy(dst, src, scale=1.0):
                    return act.activation(dst, src, ACT.Copy, scale=scale)

                def split_to(u):
                    while p.u <= min(u, U0 - 1):
                        n = p.u
                        act.wait_ge(raw_loaded[n % RAW], 16 * (n // RAW + 1))
                        if n >= SPL:
                            act.wait_ge(s["unit_used"], n - SPL + 1)
                        size = units[n][2] * units[n][4]
                        copy(whi[n % SPL][:, 0:size], raw[n % RAW][:, 0:size]).then_inc(s["hi_ready"], 1)
                        p.u += 1

                def sumsq(src, junk, c):
                    for t in range(NT):
                        act.activation(junk[:, t, c * C:(c + 1) * C], src[:, t, c * C:(c + 1) * C], ACT.Square,
                                       accum_out=ss[:, p.n, c, t:t + 1]).then_inc(s["sumsq_ready"], 1)

                def x_sumsq():
                    for c in range(2):
                        n = p.c - 2 + c
                        act.wait_ge(pair_free[n % 3], u_free(n))
                        sumsq(x, xn, c)
                    p.n += 1

                def evac_norm(dst, row, full=False):
                    for kk in range(KD // 2):
                        act.wait_ge(s["tp_done"], p.q + 1)
                        src = bank(6 + p.q % 2).rearrange("p (k t) -> p k t", k=2)
                        for k in range(2):
                            ins = copy(dst[:, 2 * kk + k, :], src[:, k, :], cT[:, row + 2 * kk + k:row + 2 * kk + k + 1])
                        if full:
                            ins.then_inc(tp_free[p.q % 2], 1)
                        else:
                            ins.then_inc(s["hi_evac"], 1)
                        p.q += 1

                def chunk_in(ue):
                    split_to(ue + 2)
                    act.wait_ge(s["unit_used"], ue + 1)

                mem_junk = Bl[:, :, :].rearrange("p a b -> p (a b)").rearrange("p (t d) -> p t d", t=NT)
                rows_src = [("g_mix", G_MIX), ("g_xattn", G_XATTN), ("g_mem", G_MEM), ("g_ffn", G_FFN)]
                for n, r in rows_src:
                    act.dma_start(rows[r:r + DEPTH * KD, :], a[n].rearrange("l (k p) -> (l k) p", p=P)
                                  ).then_inc(s["const_loaded"], 16)
                act.wait_ge(s["setup_done"], 1)
                act.dma_start(rows[R_CONV:R_SCALE, :], a["conv_w"].rearrange("l j (g p) -> (l j g) p", p=P)
                              ).then_inc(s["const_loaded"], 16)
                act.dma_start(rows[R_SCALE:ROWS, :], a["pool_scale"].rearrange("l (g p) -> (l g) p", p=P)
                              ).then_inc(s["const_loaded"], 16)
                act.wait_ge(s["mem_loaded"], 16)
                for c in range(2):
                    sumsq(xm, mem_junk, c)
                p.n += 1
                split_to(0)
                act.wait_ge(s["x_loaded"], 16)
                for c in range(2):
                    sumsq(x, xn, c)
                p.n += 1
                act.wait_ge(s["consts_done"], 1)
                copy(cT[:], bank(7)[:, 0:ROWS]).then_inc(s["consts_used"], 1)
                act.wait_ge(s["consts_used"], 1)
                evac_norm(Mh, G_MEM)
                ue = 1
                for c in range(2):
                    chunk_in(ue)
                    copy(kT[:, 4 * c:4 * c + 4, :], tiles_of(p.c)).then_inc(pair_free[p.c % 3], 1)
                    p.c += 1
                    ue += 2
                evac_norm(Ah, G_MIX)
                chunk_in(ue)
                copy(cols(vv, 0), pair(p.c).rearrange("p (t n) -> p t n", t=NT)).then_inc(pair_free[p.c % 3], 1)
                p.c += 1
                for l in range(DEPTH):
                    ue += 2
                    chunk_in(ue)
                    copy(up[:, :, PAD:], tiles_of(p.c)).then_inc(pair_free[p.c % 3], 1)
                    p.c += 1
                    ue += 2
                    chunk_in(ue)
                    copy(cg[:, :, :], tiles_of(p.c)).then_inc(pair_free[p.c % 3], 1)
                    p.c += 1
                    ue += 2
                    chunk_in(ue)
                    copy(bg[:, :, :], tiles_of(p.c)).then_inc(pair_free[p.c % 3], 1)
                    p.c += 2
                    ue += 2
                    for i in range(4):
                        ue += 2
                        chunk_in(ue)
                        act.activation(gT[:, 4 * i:4 * i + 4, :], tiles_of(p.c), ACT.Sigmoid
                                       ).then_inc(pair_free[p.c % 3], 1)
                        p.c += 1
                        if i == 1:
                            act.wait_ge(s["conv_ready"], l + 1)
                            copy(Bh[:, 4:8, :], cg[:, :, :]).then_inc(s["hi_evac"], 1)
                            split_to(ue + 3)
                            act.wait_ge(s["group_done"], l + 1)
                            for g in range(NG):
                                r = R_SCALE + l * NG + g
                                ins = copy(Bh[:, g, :], tiles_of(p.c)[:, g, :], cT[:, r:r + 1])
                            ins.then_inc(s["hi_evac"], 1)
                            p.c += 1
                    ue += 2
                    p.c += 2
                    for c in range(2):
                        split_to(ue + 3 + c)
                        act.wait_ge(s["merged_f"], 2 * l + c + 1)
                        copy(Ah[:, 4 * c:4 * c + 4, :], gT[:, 4 * c:4 * c + 4, :]).then_inc(s["hi_evac"], 1)
                        p.c += 1
                    ue += 2
                    ue += 2
                    split_to(ue + 2)
                    ue += 2
                    split_to(ue + 2)
                    p.c += 2
                    x_sumsq()
                    ue += 2
                    chunk_in(ue)
                    copy(cols(vv, 1), pair(p.c).rearrange("p (t n) -> p t n", t=NT)).then_inc(pair_free[p.c % 3], 1)
                    p.c += 1
                    evac_norm(Ah, G_XATTN + l * KD)
                    for c in range(2):
                        ue += 2
                        chunk_in(ue)
                        copy(qT[:, 4 * c:4 * c + 4, :], tiles_of(p.c), float(HD) ** -0.5
                             ).then_inc(pair_free[p.c % 3], 1)
                        p.c += 1
                    for h in range(NH):
                        act.wait_ge(s["max_ready"], NH * l + h + 1)
                        src = bank(2 * ((p.c + h // 2) % 3) + h % 2).rearrange("p (t m) -> p t m", t=NT)
                        for t in range(NT):
                            ins = act.activation(pr[:, h, t, :], src[:, t, :], ACT.Exp, bias=nmx[:, l, h, t:t + 1],
                                                 accum_out=sm[:, l, h, t:t + 1])
                        ins.then_inc(s["exp_done"], 1)
                    p.c += 2

                    def probs_t(h):
                        act.wait_ge(s["tp_done"], p.q + 1)
                        copy(pT[:, h, :, :], bank(6 + p.q % 2).rearrange("p (m t) -> p m t", m=NT)
                             ).then_inc(tp_free[p.q % 2], 1)
                        p.q += 1

                    def o_hi(h):
                        act.wait_ge(s["o_done"], NH * l + h + 1)
                        src = bank(2 * ((p.c + h // 2) % 3) + h % 2).rearrange("p (d t) -> p d t", d=2)
                        copy(Ah[:, 2 * h:2 * h + 2, :], src).then_inc(s["hi_evac"], 1)

                    probs_t(0)
                    for h in range(1, NH):
                        probs_t(h)
                        o_hi(h - 1)
                    o_hi(NH - 1)
                    p.c += 2
                    ue += 2
                    split_to(ue + 2)
                    p.c += 2
                    if l == 0:
                        act.wait_ge(s["mem_loaded"], 32)
                        for c in range(2):
                            sumsq(xm, mem_junk, c)
                        p.n += 1
                        evac_norm(Mh, G_MEM + KD)
                    ue += 2
                    split_to(ue + 2)
                    x_sumsq()
                    if l == 0:
                        for c in range(2):
                            ue += 2
                            chunk_in(ue)
                            copy(kT[:, 4 * c:4 * c + 4, :], tiles_of(p.c)).then_inc(pair_free[p.c % 3], 1)
                            p.c += 1
                        evac_norm(Ah, G_FFN)
                        for f in range(2):
                            for i, (c0, n) in enumerate(FCH):
                                nf = n // P
                                ue += 2
                                chunk_in(ue)
                                act.activation(st2[i % 2][:, 0:nf, :], tiles_of(p.c, nf), ACT.Silu
                                               ).then_inc(pair_free[p.c % 3], 1)
                                p.c += 2
                                ue += 2
                                split_to(ue + 2)
                                act.wait_ge(pair_free[(p.c - 1) % 3], u_free(p.c - 1))
                                copy(Fh[:, 4 * i:4 * i + nf, :], st2[i % 2][:, 0:nf, :]).then_inc(s["hi_evac"], 1)
                            for c in range(2):
                                ue += 3
                                split_to(ue + 2)
                                p.c += 1
                        x_sumsq()
                        ue += 2
                        chunk_in(ue)
                        copy(cols(vv, 0), pair(p.c).rearrange("p (t n) -> p t n", t=NT)).then_inc(pair_free[p.c % 3], 1)
                        p.c += 1
                        evac_norm(Ah, G_MIX + KD)
                    else:
                        evac_norm(hTf, G_FFN + KD, full=True)
                for t in range(NT):
                    act.wait_ge(s["hg_ready"], t + 1)
                    copy(hth[:, t, :], hg[:, t, :]).then_inc(s["hgh_ready"], 1)
                act.wait_ge(s["sel_ready"], 1)
                act.activation(rc[3][:], rc[2][:], ACT.Exp).then_inc(s["exp2_done"], 1)

                def expert_hi(i, v):
                    u = U0 + i
                    act.wait_ge(raw_loaded[u % RAW], v * (16 * BODY // RAW) + 16 * (u // RAW + 1))
                    act.wait_ge(s["unit_used"], v * BODY + (u - SPL + 1))
                    copy(whi[u % SPL][:], raw[u % RAW][:]).then_inc(s["hi_ready"], 1)

                def gathered_hi(n):
                    act.wait_ge(s["g_done"], n)
                    copy(heh, ps[:, 2:4, :].rearrange("p a (k c) -> p (a k) c", c=P)).then_inc(s["hehi_ready"], 1)

                def act_hi(j, v):
                    act.wait_ge(s["t_done"], v * NJ + (j + 1))
                    copy(aTh[j % 2], bank(6).rearrange("p (f c) -> p f c", c=P)).then_inc(s["acthi_ready"], 1)

                gathered_hi(1)
                act.wait_ge(s["visits_ready"], 1)
                visits = act.value_load(nvis[0:1, 0:1], min_val=NE, max_val=2 * NE)
                act.wait_ge(s["zero_done"], 1)
                with act.Fori(0, visits) as v:
                    for i in range(BODY):
                        expert_hi(i, v)
                        if i == 1:
                            act.wait_ge(s["unit_used"], v * BODY + U0)
                            copy(yh, ps[:, 4:6, :].rearrange("p a b -> p (a b)"), gc[:, 0:1]).then_inc(s["yhi_ready"], 1)
                        for j in range(NJ):
                            if i == gu_start(j) + 3:
                                act.wait_ge(s["unit_used"], v * BODY + (U0 + gu_start(j) + 2))
                                if j:
                                    act.wait_ge(s["act_ready"], v * NJ + j)
                                act.activation(silu_t[:], bank(2 * (j % 2)), ACT.Silu).then_inc(s["silu_ready"], 1)
                                if j:
                                    act_hi(j - 1, v)
                    act_hi(NJ - 1, v)
                    gathered_hi(v + 2)

            @block.vector
            def _(dve):
                p = At()
                chain = [0]

                def link(ins):
                    chain[0] += 1
                    ins.then_inc(s["dve_chain"], 1)
                    dve.wait_ge(s["dve_chain"], chain[0])

                def split_to(u):
                    while p.u <= min(u, U0 - 1):
                        n = p.u
                        dve.wait_ge(s["hi_ready"], n + 1)
                        size = units[n][2] * units[n][4]
                        dve.tensor_tensor(wlo[n % SPL][:, 0:size], raw[n % RAW][:, 0:size],
                                          whi[n % SPL][:, 0:size].bitcast(F32), ALU.subtract).then_inc(s["lo_ready"], 1)
                        p.u += 1

                def minus(dst, src, hi):
                    return dve.tensor_tensor(dst, src, hi.bitcast(F32), ALU.subtract)

                def hi_wait():
                    p.h += 1
                    dve.wait_ge(s["hi_evac"], p.h)

                def normalize(src, dst):
                    dve.wait_ge(s["rstd_ready"], p.n + 1)
                    for t in range(NT):
                        dve.tensor_scalar(dst[:, t, :], src[:, t, :], rstd[:, p.n, t:t + 1], None, ALU.mult
                                          ).then_inc(s["xn_ready"], 1)
                    p.n += 1

                def evac_norm(dst, hi, row):
                    for kk in range(KD // 2):
                        hi_wait()
                        src = bank(6 + p.q % 2).rearrange("p (k t) -> p k t", k=2)
                        for k in range(2):
                            n = 2 * kk + k
                            ins = dve.scalar_tensor_tensor(out=dst[:, n, :], in0=src[:, k, :],
                                                           scalar=cT[:, row + n:row + n + 1],
                                                           in1=hi[:, n, :].bitcast(F32), op0=ALU.mult, op1=ALU.subtract)
                        ins.then_inc(tp_free[p.q % 2], 1)
                        p.q += 1

                def x_add(ue):
                    split_to(ue + 2)
                    dve.wait_ge(s["unit_used"], ue + 1)
                    c = x_add.n % 2
                    x_add.n += 1
                    dve.tensor_tensor(cols(x, c), cols(x, c), pair(p.c).rearrange("p (t n) -> p t n", t=NT), ALU.add
                                      ).then_inc(pair_free[p.c % 3], 1)
                    p.c += 1
                x_add.n = 0

                def free(c):
                    return pair_free[c % 3]

                dve.wait_ge(s["setup_done"], 1)
                link(dve.reciprocal(inv[:], inv[:]))
                normalize(xm, xm)
                split_to(0)
                normalize(x, xn)
                dve.wait_ge(s["consts_used"], 1)
                evac_norm(Ml, Mh, G_MEM)
                ue = 3
                split_to(ue + 2)
                p.c += 2
                evac_norm(Al, Ah, G_MIX)
                ue += 2
                split_to(ue + 2)
                p.c += 1
                for l in range(DEPTH):
                    ue += 2
                    split_to(ue + 2)
                    dve.wait_ge(pair_free[p.c % 3], u_free(p.c))
                    dve.wait_ge(s["pads_ready"], l + 1)
                    E = PAD + SEQ
                    link(dve.tensor_tensor(s1[:, :, 1:], up[:, :, 1:], up[:, :, 0:E - 1], ALU.add))
                    link(dve.tensor_tensor(s2[:, 1:, 3:], s1[:, 1:, 3:], s1[:, 1:, 1:E - 2], ALU.add))
                    ue += 2
                    split_to(ue + 2)
                    link(dve.tensor_tensor(s1[:, 2:, 7:], s2[:, 2:, 7:], s2[:, 2:, 3:E - 4], ALU.add))
                    link(dve.tensor_tensor(s2[:, 3:, PAD:], s1[:, 3:, PAD:], s1[:, 3:, PAD - 8:E - 8], ALU.add))
                    for g, w in enumerate(WINDOWS):
                        src = (s1, s2)[g % 2]
                        last = dve.scalar_tensor_tensor(out=pp[:, g, :], in0=src[:, g, PAD:], scalar=1.0 / w,
                                                        in1=up[:, g, PAD:], op0=ALU.mult, op1=ALU.subtract)
                    link(last)
                    ue += 2
                    split_to(ue + 2)
                    for g in range(NG):
                        src = (s1, s2)[g % 2]
                        last = dve.tensor_tensor(pp[:, g, 0:PAD], src[:, g, PAD:2 * PAD], inv[:, g, :], ALU.mult)
                    link(last)
                    dve.tensor_tensor(pp[:, :, 0:PAD], pp[:, :, 0:PAD], up[:, :, PAD:2 * PAD], ALU.subtract
                                      ).then_inc(s["pooled_ready"], 1)
                    p.c += 3
                    ue += 2
                    split_to(ue + 2)
                    dve.wait_ge(s["unit_used"], ue + 1)
                    dve.wait_ge(pair_free[(p.c - 2) % 3], u_free(p.c - 2))
                    dve.wait_ge(pair_free[(p.c - 1) % 3], u_free(p.c - 1))
                    ins = dve.tensor_tensor(zc[:, :, CK - 1:], cg[:, :, :], tiles_of(p.c), ALU.mult)
                    ins.then_inc(free(p.c), 1)
                    dve.wait_ge(free(p.c), u_free(p.c))
                    p.c += 1
                    for j in range(CK):
                        for g in range(NG):
                            r = R_CONV + (l * CK + j) * NG + g
                            w = cT[:, r:r + 1]
                            if j == 0:
                                last = dve.tensor_scalar(cg[:, g, :], zc[:, g, 0:SEQ], w, None, ALU.mult)
                            else:
                                last = dve.scalar_tensor_tensor(out=cg[:, g, :], in0=zc[:, g, j:j + SEQ], scalar=w,
                                                                in1=cg[:, g, :], op0=ALU.mult, op1=ALU.add)
                        link(last)
                    dve.tensor_tensor(cg[:], cg[:], bg[:], ALU.mult).then_inc(s["conv_ready"], 1)
                    ue += 4
                    split_to(ue + 2)
                    hi_wait()
                    minus(Bl[:, 4:8, :], cg[:], Bh[:, 4:8, :]).then_inc(s["yc_ready"], 1)
                    p.c += 2
                    split_to(ue + 3)
                    hi_wait()
                    for g in range(NG):
                        r = R_SCALE + l * NG + g
                        ins = dve.scalar_tensor_tensor(out=Bl[:, g, :], in0=tiles_of(p.c)[:, g, :], scalar=cT[:, r:r + 1],
                                                       in1=Bh[:, g, :].bitcast(F32), op0=ALU.mult, op1=ALU.subtract)
                    ins.then_inc(free(p.c), 1)
                    p.c += 1
                    ue += 4
                    split_to(ue + 2)
                    p.c += 2
                    for c in range(4):
                        ue += 1
                        split_to(ue + 2)
                        dve.wait_ge(s["unit_used"], ue + 1)
                        if c == 0:
                            dve.wait_ge(free(p.c - 1), u_free(p.c - 1))
                        g = gT[:, 4 * c:4 * c + 4, :]
                        ins = dve.tensor_tensor(g, g, tiles_of(p.c), ALU.mult)
                        ins.then_inc(free(p.c), 1)
                        p.c += 1
                        if c >= 2:
                            dve.wait_ge(free(p.c - 1), u_free(p.c - 1))
                            m = gT[:, 4 * (c - 2):4 * (c - 2) + 4, :]
                            dve.tensor_tensor(m, m, g, ALU.add).then_inc(s["merged_f"], 1)
                            hi_wait()
                            minus(Al[:, 4 * (c - 2):4 * (c - 2) + 4, :], m, Ah[:, 4 * (c - 2):4 * (c - 2) + 4, :]
                                  ).then_inc(s["merged_ready"], 1)
                    for c in range(2):
                        ue += 2
                        x_add(ue)
                    normalize(x, xn)
                    ue += 2
                    split_to(ue + 2)
                    p.c += 1
                    evac_norm(Al, Ah, G_XATTN + l * KD)
                    ue += 4
                    split_to(ue + 2)
                    p.c += 2
                    for h in range(NH):
                        dve.wait_ge(s["scores_done"], NH * l + h + 1)
                        src = bank(2 * ((p.c + h // 2) % 3) + h % 2).rearrange("p (t m) -> p t m", t=NT)
                        link(dve.tensor_reduce(mx[:, l, h, :], src, AX_X, ALU.max))
                        dve.tensor_scalar(nmx[:, l, h, :], mx[:, l, h, :], -1.0, None, ALU.mult
                                          ).then_inc(s["max_ready"], 1)
                    for h in range(NH):
                        dve.wait_ge(s["exp_done"], NH * l + h + 1)
                        link(dve.reciprocal(rs[:, l, h, :], sm[:, l, h, :]))
                        for t in range(NT):
                            ins = dve.tensor_scalar(pr[:, h, t, :], pr[:, h, t, :], rs[:, l, h, t:t + 1], None, ALU.mult)
                            if t == 0 and h % 2:
                                ins.then_inc(pair_free[(p.c + h // 2) % 3], 1)
                        ins.then_inc(s["probs_ready"], 1)
                    p.c += 2
                    p.q += NH
                    for h in range(NH):
                        hi_wait()
                        src = bank(2 * ((p.c + h // 2) % 3) + h % 2).rearrange("p (d t) -> p d t", d=2)
                        ins = minus(Al[:, 2 * h:2 * h + 2, :], src, Ah[:, 2 * h:2 * h + 2, :])
                        ins.then_inc(pair_free[(p.c + h // 2) % 3] if h % 2 else s["o_ready"], 1)
                    p.c += 2
                    ue += 2
                    if l == 0:
                        split_to(ue + 2)
                        normalize(xm, xm)
                        c_now = p.c
                        x_add(ue)
                        evac_norm(Ml, Mh, G_MEM + KD)
                    else:
                        x_add(ue)
                    ue += 2
                    x_add(ue)
                    normalize(x, xn)
                    if l == 0:
                        for c in range(2):
                            ue += 2
                            split_to(ue + 2)
                            p.c += 1
                        evac_norm(Al, Ah, G_FFN)
                        for f in range(2):
                            for i, (c0, n) in enumerate(FCH):
                                nf = n // P
                                ue += 2
                                split_to(ue + 2)
                                ue += 2
                                split_to(ue + 2)
                                dve.wait_ge(free(p.c), u_free(p.c))
                                p.c += 1
                                dve.wait_ge(s["unit_used"], ue + 1)
                                t_ = st2[i % 2][:, 0:nf, :]
                                ins = dve.tensor_tensor(t_, t_, tiles_of(p.c, nf), ALU.mult)
                                ins.then_inc(free(p.c), 1)
                                hi_wait()
                                minus(Fl[:, 4 * i:4 * i + nf, :], t_, Fh[:, 4 * i:4 * i + nf, :]).then_inc(s["ff_ready"], 1)
                                p.c += 1
                            for c in range(2):
                                ue += 3
                                x_add(ue)
                        normalize(x, xn)
                        ue += 2
                        split_to(ue + 2)
                        p.c += 1
                        evac_norm(Al, Ah, G_MIX + KD)
                dve.wait_ge(s["gbc_loaded"], 16)
                dve.wait_ge(s["xn_ready"], 2 * p.n)
                for t in range(NT):
                    dve.tensor_tensor(hg[:, t, :], xn[:, t, :], gbc[:, :], ALU.mult).then_inc(s["hg_ready"], 1)
                for t in range(NT):
                    dve.wait_ge(s["hgh_ready"], t + 1)
                    minus(htl[:, t, :], hg[:, t, :], hth[:, t, :]).then_inc(s["htok_ready"], 1)
                dve.wait_ge(s["setup_done"], 2)
                dve.wait_ge(s["logits_done"], 1)
                link(dve.tensor_copy(lg[:], bank(0)[:, 0:NT * NE].rearrange("p (t e) -> p t e", t=NT)))

                def first_max(src, top, hot, tmp, r):
                    link(dve.tensor_reduce(top[:], src[:], AX_X, ALU.max))
                    for t in range(NT):
                        last = dve.scalar_tensor_tensor(out=tmp[:, t, :], in0=src[:, t, :], scalar=top[:, t:t + 1],
                                                        in1=rev[:, t, :], op0=ALU.is_equal, op1=ALU.mult)
                    link(last)
                    link(dve.tensor_reduce(r[:], tmp[:], AX_X, ALU.max))
                    for t in range(NT):
                        last = dve.tensor_scalar(hot[:, t, :], rev[:, t, :], r[:, t:t + 1], None, ALU.is_equal)
                    link(last)

                first_max(lg, rc[0], rt[0], rt[1], rc[4])
                link(dve.scalar_tensor_tensor(out=rt[2][:], in0=rt[0][:], scalar=-BIG, in1=lg[:], op0=ALU.mult, op1=ALU.add))
                first_max(rt[2], rc[1], rt[3], rt[1], rc[5])
                link(dve.tensor_tensor(rt[4][:], rt[0][:], rt[3][:], ALU.add))
                dve.tensor_tensor(rc[2][:], rc[1][:], rc[0][:], ALU.subtract).then_inc(s["sel_ready"], 1)
                dve.wait_ge(s["exp2_done"], 1)
                link(dve.tensor_scalar(rc[4][:], rc[3][:], 1.0, None, ALU.add))
                link(dve.reciprocal(rc[5][:], rc[4][:]))
                link(dve.tensor_tensor(rc[6][:], rc[3][:], rc[5][:], ALU.mult))
                for t in range(NT):
                    last = dve.tensor_scalar(rt[5][:, t, :], rt[3][:, t, :], rc[6][:, t:t + 1], None, ALU.mult)
                link(last)
                for t in range(NT):
                    last = dve.scalar_tensor_tensor(out=gate2[:, t, 0:NE], in0=rt[0][:, t, :], scalar=rc[5][:, t:t + 1],
                                                    in1=rt[5][:, t, :], op0=ALU.mult, op1=ALU.add)
                link(last)
                link(dve.tensor_copy(gate2[:, :, NE:2 * NE], gate2[:, :, 0:NE]))
                dve.wait_ge(s["rank_done"], 1)
                rk = bank(1)[:, 0:NT * NE].rearrange("p (t e) -> p t e", t=NT)
                link(dve.scalar_tensor_tensor(out=rt[1][:], in0=rk, scalar=1.0, in1=rt[4][:], op0=ALU.add, op1=ALU.mult))
                link(dve.tensor_scalar(posm[:, :, 0:NE], rt[1][:], -1.0, None, ALU.add))
                link(dve.tensor_scalar(posm[:, :, NE:2 * NE], rt[1][:], -1.0 - P, None, ALU.add))
                link(dve.tensor_reduce(cnt[:, 0:1], bank(1)[:, NT * NE:(NT + 1) * NE], AX_X, ALU.max))
                link(dve.tensor_scalar(cnt[:, 1:2], cnt[:, 0:1], float(P), float(NE), ALU.is_gt, ALU.mult))
                link(dve.tensor_scalar(nvis[:, 0:1], cnt[:, 1:2], float(NE), None, ALU.add))
                link(dve.tensor_scalar(nvis[:, 1:2], cnt[:, 0:1], float(P), 1.0, ALU.is_gt, ALU.add))
                dve.memset(ST[:].bitcast(F32), 0.0)
                dve.memset(gc[:], 0.0).then_inc(s["visits_ready"], 1)

                def select(col):
                    for t in range(NT):
                        ins = dve.tensor_scalar(S[:, t, :], iota[:], posm[:, t, col], None, ALU.is_equal)
                    ins.then_inc(s["s_ready"], 1)

                def gathered_lo(n):
                    dve.wait_ge(s["hehi_ready"], n)
                    minus(hel, ps[:, 2:4, :].rearrange("p a (k c) -> p (a k) c", c=P), heh).then_inc(s["he_ready"], 1)

                def expert_lo(i, v):
                    u = U0 + i
                    dve.wait_ge(s["hi_ready"], v * BODY + (u + 1))
                    minus(wlo[u % SPL][:], raw[u % RAW][:], whi[u % SPL][:]).then_inc(s["lo_ready"], 1)

                def act_lo(j, v):
                    dve.wait_ge(s["acthi_ready"], v * NJ + (j + 1))
                    minus(aTl[j % 2], bank(6).rearrange("p (f c) -> p f c", c=P), aTh[j % 2]).then_inc(s["actT_ready"], 1)

                def add_piece(n, v):
                    dve.wait_ge(s["sc_done"], v * 4 + (n + 1))
                    t, c = n // 2, n % 2
                    xs = x[:, t, c * C:(c + 1) * C]
                    dve.tensor_tensor(xs, xs, bank(6 if n == 0 else 7), ALU.add).then_inc(s["xadd_done"], 1)

                select(slice(0, 1))
                gathered_lo(1)
                visits = dve.value_load(nvis[0:1, 0:1], min_val=NE, max_val=2 * NE)
                with dve.Fori(0, visits) as v:
                    for i in range(BODY):
                        expert_lo(i, v)
                        if i == 1:
                            dve.wait_ge(s["yhi_ready"], v + 1)
                            dve.scalar_tensor_tensor(out=yl, in0=ps[:, 4:6, :].rearrange("p a b -> p (a b)"),
                                                     scalar=gc[:, 0:1], in1=yh.bitcast(F32), op0=ALU.mult,
                                                     op1=ALU.subtract).then_inc(s["y_ready"], 1)
                        for j in range(NJ):
                            if j and i == gu_start(j) + 3:
                                act_lo(j - 1, v)
                            if i == gu_start(j) + 5:
                                dve.wait_ge(s["unit_used"], v * BODY + (U0 + gu_start(j) + 4))
                                dve.wait_ge(s["silu_ready"], v * NJ + (j + 1))
                                dve.tensor_tensor(act_t[:], silu_t[:], bank(2 * (j % 2) + 1), ALU.mult
                                                  ).then_inc(s["act_ready"], 1)
                        if i == gu_start(0) + 5:
                            add_piece(0, v)
                            add_piece(1, v)
                        if i == gu_start(1) + 5:
                            add_piece(2, v)
                        if i == gu_start(2) + 5:
                            add_piece(3, v)
                        if i == gu_start(3) + 5:
                            dve.wait_ge(s["ts_done"], v + 1)
                            dve.tensor_copy(ST[:], bank(7)[:, 0:SEQ])
                            dve.tensor_copy(gc[:], bank(7)[:, SEQ:SEQ + 1]).then_inc(s["st_ready"], 1)
                            select(bass.ds(v + 1, 1))
                    act_lo(NJ - 1, v)
                    gathered_lo(v + 2)

            @block.tensor
            def _(pe):
                p = At()
                PASSES = ((0, 0), (0, 1), (1, 0))

                def take_pair():
                    if p.c >= 3:
                        pe.wait_ge(pair_free[p.c % 3], p.c // 3)

                def parts(u):
                    return unit_view(whi[u % SPL], u), unit_view(wlo[u % SPL], u)

                def chunk_t(n_units, xs, ready):
                    take_pair()
                    o = tiles_of(p.c)
                    for j in range(n_units):
                        _, k0, nk, _, nn = units[p.u]
                        w = parts(p.u)
                        pe.wait_ge(s["lo_ready"], p.u + 1)
                        for k in range(nk):
                            ready(k0 + k)
                            for d in range(nn // P):
                                for n, (wi, xi) in enumerate(PASSES):
                                    first = j == 0 and k == 0 and n == 0
                                    last = j == n_units - 1 and k == nk - 1 and n == 2
                                    ins = pe.matmul(o[:, d, :], w[wi][:, k, d * P:(d + 1) * P], xs[xi][:, k0 + k, :],
                                                    start=first and d % 2 == 0, stop=last, skip_group_check=True)
                        ins.then_inc(s["unit_used"], 1)
                        p.u += 1
                    p.c += 1

                def chunk_n(n_units, xs, ready):
                    take_pair()
                    o = pair(p.c).rearrange("p (t n) -> p t n", t=NT)
                    for j in range(n_units):
                        _, k0, nk, _, nn = units[p.u]
                        w = parts(p.u)
                        pe.wait_ge(s["lo_ready"], p.u + 1)
                        for k in range(nk):
                            ready(k0 + k)
                            for t in range(NT):
                                for n, (wi, xi) in enumerate(PASSES):
                                    ins = pe.matmul(o[:, t, 0:nn], xs[xi][:, k0 + k, t * P:(t + 1) * P], w[wi][:, k, :],
                                                    start=j == 0 and k == 0 and n == 0,
                                                    stop=j == n_units - 1 and k == nk - 1 and n == 2)
                        ins.then_inc(s["unit_used"], 1)
                        p.u += 1
                    p.c += 1

                def once(sem, value_of):
                    seen = [0]

                    def ready(k):
                        v = value_of(k)
                        if v > seen[0]:
                            pe.wait_ge(sem, v)
                            seen[0] = v
                    return ready

                def already(k):
                    return None

                def take_bank():
                    if tpn[p.q % 2]:
                        pe.wait_ge(tp_free[p.q % 2], tpn[p.q % 2])
                    tpn[p.q % 2] += 1
                tpn = [0, 0]

                def transposes(src, lo, hi):
                    pe.wait_ge(s["xn_ready"], 2 * (p.n + 1))
                    for kk in range(lo, hi):
                        take_bank()
                        b = bank(6 + p.q % 2).rearrange("p (k t) -> p k t", k=2)
                        for k in range(2):
                            for t in range(NT):
                                n = 2 * kk + k
                                ins = pe.transpose(b[:, k, t * P:(t + 1) * P], src[:, t, n * P:(n + 1) * P], ident[:])
                        ins.then_inc(s["tp_done"], 1)
                        p.q += 1
                    if hi == KD // 2:
                        p.n += 1

                def normed(q0):
                    seen = set()

                    def ready(k):
                        q = q0 + k // 2
                        if q not in seen:
                            seen.add(q)
                            pe.wait_ge(tp_free[q % 2], q // 2 + 1)
                    return ready

                MEM, XA, XB, FF = (Mh, Ml), (Ah, Al), (Bh, Bl), (Fh, Fl)
                pe.wait_ge(s["setup_done"], 1)
                pe.wait_ge(s["const_loaded"], 16 * 6)
                pe.transpose(bank(7)[:, 0:P], rows[:], ident[:]).then_inc(s["consts_done"], 1)
                pe.wait_ge(s["consts_used"], 1)
                q_mem = p.q
                transposes(xm, 0, KD // 2)
                ready = normed(q_mem)
                for c in range(2):
                    chunk_t(2, MEM, ready)
                q_h = p.q
                transposes(xn, 0, KD // 2)
                chunk_n(2, MEM, already)
                for l in range(DEPTH):
                    ready = normed(q_h)
                    for c in range(6):
                        chunk_t(2, XA, ready)
                    take_pair()
                    pe.wait_ge(s["pooled_ready"], l + 1)
                    pe.wait_ge(s["wpg_loaded"], 16 * (l + 1))
                    for g in range(NG):
                        ins = pe.matmul(tiles_of(p.c)[:, g, :], wpg[:, g, :], pp[:, g, :], start=True, stop=True)
                    ins.then_inc(s["group_done"], 1)
                    c_group = p.c
                    p.c += 1
                    for c in range(2):
                        chunk_t(2, XA, already)
                    pe.wait_ge(pair_free[c_group % 3], c_group // 3 + 1)
                    for c in range(2):
                        chunk_t(1, XB, already)
                    pe.wait_ge(s["yc_ready"], l + 1)
                    for c in range(2):
                        chunk_t(1, (Bh[:, 4:8, :], Bl[:, 4:8, :]), already)
                    ready = once(s["merged_ready"], lambda k: 2 * l + k // 4 + 1)
                    for c in range(2):
                        chunk_n(2, XA, ready)
                    chunk_n(2, MEM, already)
                    q_h = p.q
                    transposes(xn, 0, KD // 2)
                    ready = normed(q_h)
                    for c in range(2):
                        chunk_t(2, XA, ready)
                    for c in (p.c - 2, p.c - 1):
                        pe.wait_ge(pair_free[c % 3], c // 3 + 1)
                    for h in range(NH):
                        if h % 2 == 0:
                            take_pair()
                        b = bank(2 * (p.c % 3) + h % 2)
                        for t in range(NT):
                            for d in range(2):
                                ins = pe.matmul(b[:, t * SEQ:(t + 1) * SEQ], qT[:, 2 * h + d, t * P:(t + 1) * P],
                                                kT[:, 2 * h + d, :], start=d == 0, stop=d == 1)
                        ins.then_inc(s["scores_done"], 1)
                        if h % 2:
                            p.c += 1

                    def probs_t(h):
                        pe.wait_ge(s["probs_ready"], NH * l + h + 1)
                        take_bank()
                        b = bank(6 + p.q % 2).rearrange("p (m t) -> p m t", m=NT)
                        for m in range(NT):
                            for t in range(NT):
                                ins = pe.transpose(b[:, m, t * P:(t + 1) * P], pr[:, h, t, m * P:(m + 1) * P], ident[:])
                        ins.then_inc(s["tp_done"], 1)
                        p.q += 1

                    def head_out(h):
                        if h % 2 == 0:
                            take_pair()
                        q = q_p + h
                        pe.wait_ge(tp_free[q % 2], q // 2 + 1)
                        b = bank(2 * (p.c % 3) + h % 2)
                        for d in range(2):
                            for m in range(NT):
                                ins = pe.matmul(b[:, d * SEQ:(d + 1) * SEQ], vv[:, m, h * HD + d * P:h * HD + (d + 1) * P],
                                                pT[:, h, m, :], start=m == 0, stop=m == NT - 1)
                        ins.then_inc(s["o_done"], 1)
                        if h % 2:
                            p.c += 1

                    q_p = p.q
                    c_o = p.c
                    probs_t(0)
                    for h in range(1, NH):
                        probs_t(h)
                        head_out(h - 1)
                    head_out(NH - 1)
                    seen = set()

                    def ready(k):
                        h = k // 2
                        if h not in seen:
                            seen.add(h)
                            c = c_o + h // 2
                            if h % 2:
                                pe.wait_ge(pair_free[c % 3], u_free(c))
                            else:
                                pe.wait_ge(s["o_ready"], NH // 2 * l + h // 2 + 1)
                    chunk_n(2, XA, ready)
                    q_mem = p.q
                    if l == 0:
                        transposes(xm, 0, 2)
                    chunk_n(2, XA, already)
                    if l == 0:
                        transposes(xm, 2, 4)
                        ready = normed(q_mem)
                        for c in range(2):
                            chunk_t(2, MEM, ready)
                        q_h = p.q
                        transposes(xn, 0, KD // 2)
                        ready = normed(q_h)
                        for f in range(2):
                            for i in range(len(FCH)):
                                chunk_t(2, XA, ready)
                                chunk_t(2, XA, already)
                            ready = already
                            r = once(s["ff_ready"], lambda k: 3 * f + k // 4 + 1)
                            for c in range(2):
                                chunk_n(3, FF, r)
                        chunk_n(2, MEM, already)
                        q_h = p.q
                        transposes(xn, 0, KD // 2)
                    else:
                        ready = normed(p.q)
                        transposes(xn, 0, KD // 2)
                for c in range(p.c - 3, p.c):
                    pe.wait_ge(pair_free[c % 3], c // 3 + 1)
                pe.wait_ge(s["wrt_loaded"], 16)
                for t in range(NT):
                    for k in range(KD):
                        if t == 0:
                            ready(k)
                        ins = pe.matmul(bank(0)[:, t * NE:(t + 1) * NE], hTf[:, k, t * P:(t + 1) * P], wrt[:, k, :],
                                        start=k == 0, stop=k == KD - 1)
                ins.then_inc(s["logits_done"], 1)
                pe.wait_ge(s["sel_ready"], 1)
                sel = rt[4]
                pe.matmul(bank(1)[:, 0:NE], tri[:], sel[:, 0, :], start=True, stop=True)
                pe.matmul(bank(1)[:, NE:2 * NE], ones[:], sel[:, 0, :], start=True, stop=False)
                pe.matmul(bank(1)[:, NE:2 * NE], tri[:], sel[:, 1, :], start=False, stop=True)
                pe.matmul(bank(1)[:, 2 * NE:3 * NE], ones[:], sel[:, 0, :], start=True, stop=False)
                pe.matmul(bank(1)[:, 2 * NE:3 * NE], ones[:], sel[:, 1, :], start=False, stop=True
                          ).then_inc(s["rank_done"], 1)
                pe.wait_ge(s["visits_ready"], 1)
                for b in (4, 5):
                    for n in range(2):
                        ins = pe.matmul(bank(b)[:, n * SEQ:(n + 1) * SEQ], ST[:, 0:P], ST[:, :], start=True, stop=True)
                ins.then_inc(s["zero_done"], 1)

                def gather(n):
                    pe.wait_ge(s["s_ready"], n)
                    for k in range(KD):
                        o = bank(2 + k // 4)[:, (k % 4) * P:(k % 4 + 1) * P]
                        for t in range(NT):
                            for m, h in enumerate((hth, htl)):
                                ins = pe.matmul(o, h[:, t, k * P:(k + 1) * P], S[:, t, :], start=t == 0 and m == 0,
                                                stop=t == NT - 1 and m == 1)
                    ins.then_inc(s["g_done"], 1)

                def gate_up(j, first, o, v):
                    for part in range(2):
                        u = U0 + gu_start(j) + first + part
                        pe.wait_ge(s["lo_ready"], v * BODY + (u + 1))
                        w = [t[u % SPL][:, :].rearrange("p (k n) -> p k n", k=4) for t in (whi, wlo)]
                        for k in range(4):
                            for n, (wi, xi) in enumerate(PASSES):
                                ins = pe.matmul(o, (heh, hel)[xi][:, 4 * part + k, :], w[wi][:, k, :],
                                                start=part == 0 and k == 0 and n == 0,
                                                stop=part == 1 and k == 3 and n == 2)
                        ins.then_inc(s["unit_used"], 1)

                def act_t_(j, v):
                    pe.wait_ge(s["act_ready"], v * NJ + (j + 1))
                    if j == 0:
                        pe.wait_ge(s["xadd_done"], v * 4 + 1)
                    for f in range(4):
                        ins = pe.transpose(bank(6)[:, f * P:(f + 1) * P], act_t[:, f * P:(f + 1) * P], ident[:])
                    ins.then_inc(s["t_done"], 1)

                def down(j, i0, v):
                    pe.wait_ge(s["actT_ready"], v * NJ + (j + 1))
                    for part in range(2):
                        u = U0 + i0 + part
                        pe.wait_ge(s["lo_ready"], v * BODY + (u + 1))
                        w = [t[u % SPL][:, :].rearrange("p (k n) -> p k n", k=2) for t in (whi, wlo)]
                        for k in range(2):
                            f = 2 * part + k
                            for c in range(2):
                                for n, (wi, xi) in enumerate(PASSES):
                                    ins = pe.matmul(bank(4 + c), (aTh, aTl)[xi][j % 2][:, f, :],
                                                    w[wi][:, k, c * C:(c + 1) * C],
                                                    start=j == 0 and f == 0 and n == 0,
                                                    stop=j == NJ - 1 and f == 3 and n == 2)
                        ins.then_inc(s["unit_used"], 1)

                def scatter(n, v):
                    t, c = n // 2, n % 2
                    for m, y in enumerate((yh, yl)):
                        ins = pe.matmul(bank(6 if n == 0 else 7), ST[:, t * P:(t + 1) * P], y[:, c * C:(c + 1) * C],
                                        start=m == 0, stop=m == 1)
                    ins.then_inc(s["sc_done"], 1)

                for t in range(NT):
                    pe.wait_ge(s["htok_ready"], t + 1)
                gather(1)
                visits = pe.value_load(nvis[0:1, 0:1], min_val=NE, max_val=2 * NE)
                with pe.Fori(0, visits) as v:
                    for j in range(NJ):
                        if j == 0:
                            pe.wait_ge(s["he_ready"], v + 1)
                        gate_up(j, 0, bank(2 * (j % 2)), v)
                        if j:
                            act_t_(j - 1, v)
                        gate_up(j, 2, bank(2 * (j % 2) + 1), v)
                        if j == 0:
                            pe.wait_ge(s["y_ready"], v + 1)
                            scatter(0, v)
                            scatter(1, v)
                        elif j < 3:
                            pe.wait_ge(s["xadd_done"], v * 4 + (j + 1))
                            scatter(j + 1, v)
                        elif j == 3:
                            pe.wait_ge(s["xadd_done"], v * 4 + 4)
                            for t in range(NT):
                                pe.transpose(bank(7)[:, t * P:(t + 1) * P], S[:, t, :].bitcast(F32), ident[:])
                            for t in range(NT):
                                ins = pe.matmul(bank(7)[:, SEQ:SEQ + 1], S[:, t, :].bitcast(F32),
                                                gate2[:, t, bass.ds(v, 1)], start=t == 0, stop=t == NT - 1)
                            ins.then_inc(s["ts_done"], 1)
                        if j:
                            down(j - 1, gu_start(j) + 4, v)
                    act_t_(NJ - 1, v)
                    gather(v + 2)
                    down(NJ - 1, BODY - 2, v)

        with nc.Block() as block:
            @block.scalar
            def _(act):
                act.activation(yh, ps[:, 4:6, :].rearrange("p a b -> p (a b)"), ACT.Copy, scale=gc[:, 0:1]
                               ).then_inc(s["tail_y"], 1)
                for t in range(NT):
                    act.wait_ge(s["tail_x"], 2 * t + 2)
                    act.activation(xn[:, t, :], x[:, t, :], ACT.Square, accum_out=ss[:, 8, 0, t:t + 1]
                                   ).then_inc(s["tail_ss"], 1)

            @block.vector
            def _(dve):
                dve.wait_ge(s["tail_y"], 1)
                dve.scalar_tensor_tensor(out=yl, in0=ps[:, 4:6, :].rearrange("p a b -> p (a b)"), scalar=gc[:, 0:1],
                                         in1=yh.bitcast(F32), op0=ALU.mult, op1=ALU.subtract).then_inc(s["tail_yl"], 1)
                for n in range(4):
                    dve.wait_ge(s["tail_sc"], n + 1)
                    xs = x[:, n // 2, n % 2 * C:(n % 2 + 1) * C]
                    dve.tensor_tensor(xs, xs, bank(n), ALU.add).then_inc(s["tail_x"], 1)
                dve.wait_ge(s["tail_r"], 2)
                dve.wait_ge(s["gfin_loaded"], 16)
                for t in range(NT):
                    dve.scalar_tensor_tensor(out=hg[:, t, :], in0=x[:, t, :], scalar=rstd[:, 8, t:t + 1], in1=gbc[:],
                                             op0=ALU.mult, op1=ALU.mult).then_inc(s["tail_o"], 1)

            @block.gpsimd
            def _(pool):
                pool.wait_ge(s["tail_ss"], 2)
                pool.tensor_scalar(sst[:, 8, 1, :], ss[:, 8, 0, :], 1.0 / D, EPS, ALU.mult, ALU.add
                                   ).then_inc(s["tail_r"], 1)
                pool.wait_ge(s["tail_r"], 1)
                pool.tensor_tensor(rstd[:, 8, :], sst[:, 8, 1, :], mhalf[:], ALU.pow).then_inc(s["tail_r"], 1)

            @block.tensor
            def _(pe):
                pe.wait_ge(s["tail_yl"], 1)
                for n in range(4):
                    t, c = n // 2, n % 2
                    for m, y in enumerate((yh, yl)):
                        ins = pe.matmul(bank(n), ST[:, t * P:(t + 1) * P], y[:, c * C:(c + 1) * C],
                                        start=m == 0, stop=m == 1)
                    ins.then_inc(s["tail_sc"], 1)

            @block.sync
            def _(sp):
                for t in range(NT):
                    sp.wait_ge(s["tail_o"], t + 1)
                    sp.dma_start(out[0, t * P:(t + 1) * P, :], hg[:, t, :]).then_inc(s["stored"], 16)
                sp.wait_ge(s["stored"], 16 * NT)


def kernel(**inputs):
    import numpy as _np
    import concourse.bacc as _bacc
    from concourse import mybir as _mybir
    from concourse.bass_utils import run_bass_kernel_spmd as _run

    nc = _bacc.Bacc("TRN2", target_bir_lowering=False, num_devices=1, dynamic_dma_scratch_size=1024)
    arrays, aps = {}, {}
    for name, value in inputs.items():
        arrays[f"in_{name}"] = _np.ascontiguousarray(value)
        aps[name] = nc.dram_tensor(f"in_{name}", arrays[f"in_{name}"].shape, _mybir.dt.from_np(arrays[f"in_{name}"].dtype),
                                   kind="ExternalInput").ap()
    out = nc.dram_tensor("out_0", inputs["x"].shape, _mybir.dt.from_np(_np.dtype("float32")), kind="ExternalOutput").ap()
    trunk(nc, aps, out)
    r = _run(nc, [arrays], core_ids=[0])
    return r.results[0]["out_0"]
```

```python
import concourse.bass as bass
from concourse import mybir

F32 = mybir.dt.float32
F32R = mybir.dt.float32r
I32 = mybir.dt.int32
ALU = mybir.AluOpType
ACT = mybir.ActivationFunctionType
AX_X = mybir.AxisListType.X

P = 128
EPS = 1e-6
UNIT = 2048
RAW = 6
SPL = 3
MR = 14
AHEAD = 3
BIG = 3.0e38


def trunk(nc, a, out):
    SEQ, D = a["x"].shape[1:]
    DEPTH = a["w_in"].shape[0]
    NT, KD = SEQ // P, D // P
    HALF = D // 2
    NG = HALF // P
    DFF = a["w_ff_gate"].shape[2]
    NE, DFE = a["w_e_gate"].shape[1], a["w_e_gate"].shape[3]
    NH = 4
    HD = D // NH
    C = 512
    NJ = DFE // C
    BODY = 6 * NJ
    WINDOWS = (2, 4, 8, 16)
    PAD = max(WINDOWS)
    CK = a["conv_w"].shape[1]
    FH = DFF // 2
    FT = FH // P
    FCH = [(c, min(C, FH - c)) for c in range(0, FH, C)]
    assert NT == 2 and KD == 8 and NG == 4 and DEPTH == 2 and FH % P == 0 and BODY % MR == 0

    units = []

    def add_units(w, kts, col, cols):
        per = UNIT // cols if cols == C else 4
        for k in range(0, kts, per):
            units.append((w, k, min(per, kts - k), col, cols))

    def add_square(w, chunks=(0, 1)):
        for c in chunks:
            add_units(w, KD, c * C, C)

    add_square(a["w_xk"][0])
    add_square(a["w_xv"][0], (0,))
    z_start, q_start, mix_start = [], [], []
    for l in range(DEPTH):
        z_start.append(len(units))
        for c in range(a["w_in"].shape[2] // C):
            add_units(a["w_in"][l], KD, c * C, C)
        for w in (a["w_pool_out"][l], a["w_conv_out"][l]):
            for c in range(2):
                add_units(w, NG, c * C, C)
        mix_start.append(len(units))
        add_square(a["w_mix_out"][l])
        add_square(a["w_xv"][l], (1,))
        q_start.append(len(units))
        add_square(a["w_xq"][l])
        add_square(a["w_xo"][l])
        if l == 0:
            add_square(a["w_xk"][1])
            for f in range(2):
                for c, n in FCH:
                    add_units(a["w_ff_gate"][0], KD, f * FH + c, n)
                    add_units(a["w_ff_up"][0], KD, f * FH + c, n)
                for c in range(2):
                    add_units(a["w_ff_down"][0][f * FH:(f + 1) * FH, :], FT, c * C, C)
            add_square(a["w_xv"][1], (0,))
    U0 = len(units)

    G_MIX, G_XATTN, G_MEM, G_FFN = (i * DEPTH * KD for i in range(4))
    R_CONV = 4 * DEPTH * KD
    R_SCALE = R_CONV + DEPTH * CK * NG
    ROWS = R_SCALE + DEPTH * NG

    assert ROWS % 32 == 0

    base = (nc.sbuf_base + 63) // 64 * 64
    at = {"top": base}
    place_of = {}

    def place(name, shape, dt, where=None):
        size = 4
        for s in shape[1:]:
            size *= s
        if where is None:
            where = at["top"]
            at["top"] += (size + 63) // 64 * 64
        place_of[name] = where
        return nc.alloc_sbuf_tensor_at(name, shape, dt, offset=where)

    raw = [place(f"raw{i}", [P, UNIT], F32) for i in range(RAW)]
    whi = [place(f"whi{i}", [P, UNIT], F32R) for i in range(SPL)]
    wlo = [place(f"wlo{i}", [P, UNIT], F32R) for i in range(SPL)]
    x = place("x_res", [P, NT, D], F32)
    Ah = place("a_hi", [P, KD, SEQ], F32R)
    Al = place("a_lo", [P, KD, SEQ], F32R)
    Bh = place("b_hi", [P, KD, SEQ], F32R)
    Bl = place("b_lo", [P, KD, SEQ], F32R)
    Mh = place("mem_hi", [P, KD, SEQ], F32R)
    Ml = place("mem_lo", [P, KD, SEQ], F32R)
    kT = place("kT", [P, KD, SEQ], F32)
    vv = place("v_tok", [P, NT, D], F32)
    moe_top = at["top"]
    gT = place("gatesT", [P, 2 * KD, SEQ], F32)
    sc = at["top"]
    at["top"] += 32768
    ident = place("ident", [P, P], F32)
    cT = place("consts_t", [P, ROWS], F32)
    inv = place("inv_count", [P, NG, PAD], F32)
    wpg = place("w_group", [P, NG, P], F32)
    wrt = place("w_rout", [P, KD, NE], F32)
    NORMS = 9
    ss = place("sumsq", [P, NORMS, 2, NT], F32)
    sst = place("sumsq_t", [P, NORMS, 2, NT], F32)
    rstd = place("rstd", [P, NORMS, NT], F32)
    mhalf = place("minus_half", [P, NT], F32)
    mx = place("max_s", [P, DEPTH, NH, NT], F32)
    nmx = place("neg_max", [P, DEPTH, NH, NT], F32)
    sm = place("sum_s", [P, DEPTH, NH, NT], F32)
    rs = place("rsum_s", [P, DEPTH, NH, NT], F32)
    assert at["top"] <= nc.sbuf_usable_end, (at["top"], nc.sbuf_usable_end)
    arena_size = at["top"] - nc.sbuf_base

    xn = place("x_norm", [P, NT, D], F32, sc)
    xm = place("mem_norm", [P, NT, D], F32, sc + 24576)
    rows = place("const_rows", [P, P], F32, sc + 8192)
    cg = place("c_gateT", [P, NG, SEQ], F32, sc)
    bg = place("b_gateT", [P, NG, SEQ], F32, sc + 4096)
    up = place("u_pool_pad", [P, NG, PAD + SEQ], F32, sc + 8192)
    s1 = place("win_sum1", [P, NG, PAD + SEQ], F32, sc + 12544)
    s2 = place("win_sum2", [P, NG, PAD + SEQ], F32, sc + 16896)
    pp = place("pooledT", [P, NG, SEQ], F32, sc + 21248)
    zc = place("conv_in_pad", [P, NG, CK - 1 + SEQ], F32, sc + 25344)
    qT = place("qT", [P, KD, SEQ], F32, sc)
    pr = place("probs", [P, NH, NT, SEQ], F32, sc + 8192)
    pT = place("probsT", [P, NH, NT, SEQ], F32, sc + 16384)
    Fh = place("ff_hi", [P, FT, SEQ], F32R, sc)
    Fl = place("ff_lo", [P, FT, SEQ], F32R, sc + FT * SEQ * 4)
    st2 = [place(f"ff_tmp{i}", [P, 4, SEQ], F32, sc + 22528 + 4096 * i) for i in range(2)]
    hg = place("h_tok", [P, NT, D], F32, sc + 8192)
    m0 = moe_top

    def moe(name, shape, dt):
        t = place(name, shape, dt, m0 + moe.off)
        n = 4
        for s in shape[1:]:
            n *= s
        moe.off += (n + 63) // 64 * 64
        assert moe.off <= 16384
        return t
    moe.off = 0
    S = moe("sel_tok", [P, NT, P], F32)
    ST = moe("sel_slot", [P, SEQ], F32R)
    gc = moe("gate_slot", [P, 1], F32)
    first_silu = moe("first_silu", [P, 1], F32)
    iota = moe("iota_slots", [P, P], F32)
    tri = moe("strict_upper", [P, P], F32)
    ones = moe("ones", [P, P], F32)
    silu_t = moe("silu_tmp", [P, C], F32)
    act_t = moe("act_tok", [P, C], F32)
    rev = moe("rev_index", [P, NT, NE], F32)
    rt = [moe(f"route{i}", [P, NT, NE], F32) for i in range(6)]
    rc = [moe(f"route_c{i}", [P, NT], F32) for i in range(8)]
    wr2 = moe("w_rout_parts", [P, KD, 2 * NE], F32R)
    lgT = moe("logitsT", [2 * NE, SEQ], F32)
    fold = moe("fold", [2 * NE, NE], F32)
    posm = moe("rank", [P, NT, 2 * NE + 1], F32)
    gate2 = moe("gate", [P, NT, 2 * NE], F32)
    gbc = moe("g_rows", [P, D], F32)
    cnt = moe("count", [P, 2], F32)
    nvis = moe("n_visits", [P, 2], I32)
    more_raw = [place(f"raw_more{i}", [P, UNIT], F32, where) for i, where in enumerate(
        (place_of["b_hi"], place_of["b_lo"], sc + 24576, place_of["kT"], place_of["v_tok"], sc + 16384,
         sc, place_of["a_lo"]))]

    def moe_raw(i):
        m = i % MR
        return raw[(U0 + m) % RAW][:] if m < RAW else more_raw[m - RAW][:]

    aTh = [Mh[:, 2 * i:2 * i + 2, :].rearrange("p a b -> p (a b)").rearrange("p (f c) -> p f c", c=P) for i in range(2)]
    aTl = [Ml[:, 2 * i:2 * i + 2, :].rearrange("p a b -> p (a b)").rearrange("p (f c) -> p f c", c=P) for i in range(2)]
    yh = Mh[:, 4:8, :].rearrange("p a b -> p (a b)")
    yl = Ml[:, 4:8, :].rearrange("p a b -> p (a b)")
    heh = Ah[:, 0:4, :].rearrange("p a b -> p (a b)").rearrange("p (k c) -> p k c", c=P)
    hel = Ah[:, 4:8, :].rearrange("p a b -> p (a b)").rearrange("p (k c) -> p k c", c=P)

    names = """const_loaded mem_loaded mem_t1_loaded x_loaded wpg_loaded wrt_loaded gbc_loaded setup_done
        consts_done consts_used hi_ready lo_ready unit_used sumsq_ready rstd_ready xn_ready tp_done hi_evac
        pads_ready pooled_ready group_done conv_ready yc_ready merged_f merged_ready scores_done max_ready
        exp_done probs_ready o_done o_ready ff_ready dve_chain pool_chain wrh_ready wrl_ready lgT_ready lg_done
        x_half count_done hg_ready logits_done hot_ready gate2_ready sel_ready rank_done exp2_done visits_ready
        zero_done t_done g_done sc_done ts_done silu_ready acthi_ready hehi_ready yhi_ready act_ready
        actT_ready he_ready y_ready xadd_done st_ready s_ready tail_y tail_yl tail_sc tail_x tail_ss tail_r
        tail_xg tail_o tail_o1 gfin_loaded stored""".split()

    import contextlib
    with contextlib.ExitStack() as ctx:
        ctx.enter_context(nc.sbuf_tensor("arena", [P, arena_size // 4], F32))
        ps = ctx.enter_context(nc.psum_tensor("ps", [P, 8, 512], F32))
        s = {n: ctx.enter_context(nc.semaphore(n)) for n in names}
        raw_loaded = [ctx.enter_context(nc.semaphore(f"raw_loaded{i}")) for i in range(RAW)]
        moe_loaded = [ctx.enter_context(nc.semaphore(f"moe_loaded{i}")) for i in range(MR)]
        pair_free = [ctx.enter_context(nc.semaphore(f"pair_free{i}")) for i in range(3)]
        tp_free = [ctx.enter_context(nc.semaphore(f"tp_free{i}")) for i in range(2)]

        def pair(c):
            b = 2 * (c % 3)
            return ps[:, b:b + 2, :].rearrange("p a b -> p (a b)")

        def tiles_of(c, n=4):
            return pair(c)[:, 0:n * SEQ].rearrange("p (d t) -> p d t", t=SEQ)

        def bank(b):
            return ps[:, b, :]

        class At:
            def __init__(self):
                self.u = self.c = self.q = self.n = self.h = 0

        def unit_view(t, u):
            _, _, nk, _, nn = units[u]
            return t[:, 0:nk * nn].rearrange("p (k n) -> p k n", k=nk)

        def cols(ap, c):
            return ap[:, :, c * C:(c + 1) * C]

        def expert_unit(i):
            if i < 4:
                return 0, ("gate", "gate", "up", "up")[i], i % 2
            j, r = divmod(i - 4, 6)
            j += 1
            if j == NJ:
                return NJ - 1, "down", r
            if r < 4:
                return j, ("gate", "gate", "up", "up")[r], r % 2
            return j - 1, "down", r - 4

        def gu_start(j):
            return 0 if j == 0 else 4 + 6 * (j - 1)

        def u_free(c):
            return c // 3 + 1

        with nc.Block() as block:

            @block.sync
            def _(sp):
                def load_unit(u):
                    w, k, nk, col, nn = units[u]
                    if u >= RAW:
                        sp.wait_ge(s["lo_ready"], u - RAW + 1)
                    sp.dma_start(unit_view(raw[u % RAW], u),
                                 w[k * P:(k + nk) * P, col:col + nn].rearrange("(k p) n -> p k n", p=P)
                                 ).then_inc(raw_loaded[u % RAW], 16)

                mem_rows = a["mem"][0].rearrange("(t p) d -> p t d", p=P)
                sp.dma_start(xm[:, 0, :], mem_rows[:, 0, :]).then_inc(s["mem_loaded"], 16)
                sp.dma_start(xm[:, 1:, :], mem_rows[:, 1:, :]).then_inc(s["mem_t1_loaded"], 16)
                for n, r in (("g_mem", G_MEM), ("g_mix", G_MIX), ("g_xattn", G_XATTN), ("g_ffn", G_FFN)):
                    sp.dma_start(rows[r:r + DEPTH * KD, :], a[n].rearrange("l (k p) -> (l k) p", p=P)
                                 ).then_inc(s["const_loaded"], 16)
                sp.dma_start(rows[R_CONV:R_SCALE, :], a["conv_w"].rearrange("l j (g p) -> (l j g) p", p=P)
                             ).then_inc(s["const_loaded"], 16)
                sp.dma_start(rows[R_SCALE:ROWS, :], a["pool_scale"].rearrange("l (g p) -> (l g) p", p=P)
                             ).then_inc(s["const_loaded"], 16)
                load_unit(0)
                load_unit(1)
                sp.dma_start(x[:], a["x"][0].rearrange("(t p) d -> p t d", p=P)).then_inc(s["x_loaded"], 16)
                load_unit(2)
                load_unit(3)
                sp.dma_start(wpg[:], a["w_pool_group"][0].rearrange("g c d -> c g d")).then_inc(s["wpg_loaded"], 16)
                sp.dma_start(wrt[:], a["w_router"][0].rearrange("(k p) e -> p k e", p=P)).then_inc(s["wrt_loaded"], 16)
                for u in range(4, U0):
                    if u == q_start[0] + 4:
                        sp.wait_ge(s["merged_ready"], 2)
                        sp.dma_start(xm[:], mem_rows).then_inc(s["mem_loaded"], 16)
                        sp.wait_ge(s["group_done"], 1)
                        sp.dma_start(wpg[:], a["w_pool_group"][1].rearrange("g c d -> c g d")).then_inc(s["wpg_loaded"], 16)
                    load_unit(u)
                sp.wait_ge(s["merged_ready"], 2 * DEPTH)
                sp.dma_start(gbc[:], a["g_ffn"][1:2, :].broadcast_to([P, D])).then_inc(s["gbc_loaded"], 16)

                def load_expert_unit(i, e):
                    t = moe_raw(i)
                    j, w, part = expert_unit(i)
                    if w == "down":
                        src = a["w_e_down"][0][bass.ds(e, 1), (j * 4 + part * 2) * P:(j * 4 + part * 2 + 2) * P, :]
                        dst = t.rearrange("p (k n) -> p k n", k=2)
                    else:
                        src = a["w_e_" + w][0][bass.ds(e, 1), part * C:(part + 1) * C, j * C:(j + 1) * C]
                        dst = t.rearrange("p (k n) -> p k n", k=4)
                    sp.dma_start(dst, src.rearrange("e (k p) n -> p (e k) n", p=P)).then_inc(moe_loaded[i % MR], 16)

                def load_rest(e, v):
                    for i in range(MR, BODY):
                        sp.wait_ge(s["lo_ready"], v * BODY + (U0 + i - MR + 1))
                        load_expert_unit(i, e)

                def load_first(e, v):
                    for i in range(MR):
                        sp.wait_ge(s["lo_ready"], v * BODY + (U0 + i - MR + 1))
                        load_expert_unit(i, e)

                for i in range(MR):
                    if i < RAW:
                        sp.wait_ge(s["lo_ready"], U0 + i - RAW + 1)
                    elif i == RAW:
                        sp.wait_ge(s["unit_used"], mix_start[-1])
                    elif i == RAW + 3:
                        sp.wait_ge(s["o_done"], NH * DEPTH)
                    elif i == MR - 2:
                        sp.wait_ge(s["tp_done"], (NORMS - 1) * KD // 2 + NH * DEPTH)
                        sp.wait_ge(s["hg_ready"], NT)
                    elif i == MR - 1:
                        sp.wait_ge(s["logits_done"], 1)
                    load_expert_unit(i, 0)
                with sp.Fori(0, NE - 1) as e:
                    load_rest(e, e)
                    load_first(e + 1, e + 1)
                load_rest(NE - 1, NE - 1)
                sp.wait_ge(s["visits_ready"], 1)
                visits = sp.value_load(nvis[0:1, 0:1], min_val=NE, max_val=2 * NE)
                with sp.If(visits > NE):
                    with sp.Fori(0, NE) as e:
                        load_first(e, e + NE)
                        load_rest(e, e + NE)
                sp.dma_start(gbc[:], a["g_final"].rearrange("(a d) -> a d", a=1).broadcast_to([P, D])
                             ).then_inc(s["gfin_loaded"], 16)

            @block.gpsimd
            def _(pool):
                chain = [0]

                def link(ins):
                    chain[0] += 1
                    ins.then_inc(s["pool_chain"], 1)
                    pool.wait_ge(s["pool_chain"], chain[0])

                link(pool.memset(ident[:], 0.0))
                link(pool.affine_select(out=ident[:], in_=ident[:], compare_op=ALU.not_equal, fill=1.0, base=0,
                                        pattern=[[-1, P]], channel_multiplier=1))
                link(pool.memset(mhalf[:], -0.5))
                link(pool.iota(inv[:, :, :], pattern=[[0, NG], [1, PAD]], base=1, channel_multiplier=0,
                               allow_small_or_imprecise_dtypes=True))
                for g, w in enumerate(WINDOWS):
                    link(pool.tensor_scalar(inv[:, g, :], inv[:, g, :], float(w), None, ALU.min))
                pool.memset(rows[ROWS:, :], 0.0).then_inc(s["setup_done"], 1)
                pool.wait_ge(s["setup_done"], 1)

                def root(n, parts):
                    pool.wait_ge(s["sumsq_ready"], parts)
                    link(pool.tensor_tensor(sst[:, n, 0, :], ss[:, n, 0, :], ss[:, n, 1, :], ALU.add))
                    link(pool.tensor_scalar(sst[:, n, 1, :], sst[:, n, 0, :], 1.0 / D, EPS, ALU.mult, ALU.add))
                    pool.tensor_tensor(rstd[:, n, :], sst[:, n, 1, :], mhalf[:], ALU.pow).then_inc(s["rstd_ready"], 1)

                def pads(u_first):
                    pool.wait_ge(s["unit_used"], u_first + 1)
                    pool.memset(up[:, :, 0:PAD], 0.0)
                    pool.memset(zc[:, :, 0:CK - 1], 0.0).then_inc(s["pads_ready"], 1)

                root(0, 4)
                root(1, 8)
                pads(z_start[0])
                for n in range(2, 6):
                    root(n, 4 * n + 4)
                pads(z_start[1])
                root(6, 28)
                pool.wait_ge(s["merged_ready"], 2 * DEPTH)
                link(pool.iota(iota[:, :], pattern=[[1, P]], base=1, channel_multiplier=0,
                               allow_small_or_imprecise_dtypes=True))
                link(pool.iota(rev[:, :, :], pattern=[[0, NT], [-1, NE]], base=NE, channel_multiplier=0,
                               allow_small_or_imprecise_dtypes=True))
                link(pool.memset(ones[:], 1.0))
                link(pool.affine_select(out=tri[:], in_=ones[:], compare_op=ALU.is_gt, fill=0.0, base=0,
                                        pattern=[[1, P]], channel_multiplier=-1))
                pool.memset(ST[:].bitcast(F32), 0.0)
                pool.memset(gc[:], 0.0)
                pool.memset(posm[:, :, 2 * NE:2 * NE + 1], -1.0).then_inc(s["setup_done"], 1)
                root(7, 32)
                pool.wait_ge(s["gbc_loaded"], 16)
                for t in range(NT):
                    pool.wait_ge(s["xn_ready"], 2 * 7 + t + 1)
                    pool.tensor_tensor(hg[:, t, :], xn[:, t, :], gbc[:, :], ALU.mult).then_inc(s["hg_ready"], 1)

            @block.scalar
            def _(act):
                p = At()

                def copy(dst, src, scale=1.0):
                    return act.activation(dst, src, ACT.Copy, scale=scale)

                def split_to(u):
                    while p.u <= min(u, U0 - 1):
                        n = p.u
                        act.wait_ge(raw_loaded[n % RAW], 16 * (n // RAW + 1))
                        if n >= SPL:
                            act.wait_ge(s["unit_used"], n - SPL + 1)
                        size = units[n][2] * units[n][4]
                        copy(whi[n % SPL][:, 0:size], raw[n % RAW][:, 0:size]).then_inc(s["hi_ready"], 1)
                        p.u += 1

                def expert_hi(i, v):
                    u = U0 + i
                    act.wait_ge(moe_loaded[i % MR], v * (16 * BODY // MR) + 16 * (i // MR + 1))
                    act.wait_ge(s["unit_used"], v * BODY + (u - SPL + 1))
                    copy(whi[u % SPL][:], moe_raw(i)).then_inc(s["hi_ready"], 1)

                def sumsq(src, junk, c, tiles=(0, 1)):
                    for t in tiles:
                        act.activation(junk[:, t, c * C:(c + 1) * C], src[:, t, c * C:(c + 1) * C], ACT.Square,
                                       accum_out=ss[:, p.n, c, t:t + 1]).then_inc(s["sumsq_ready"], 1)

                def x_sumsq():
                    act.wait_ge(pair_free[(p.c - 2) % 3], u_free(p.c - 2))
                    sumsq(x, xn, 0)
                    x_sumsq.n += 1
                    for t in range(NT):
                        if t == 0:
                            act.wait_ge(s["x_half"], x_sumsq.n)
                        else:
                            act.wait_ge(pair_free[(p.c - 1) % 3], u_free(p.c - 1))
                        act.activation(xn[:, t, C:], x[:, t, C:], ACT.Square,
                                       accum_out=ss[:, p.n, 1, t:t + 1]).then_inc(s["sumsq_ready"], 1)
                    p.n += 1
                x_sumsq.n = 0

                def evac_norm(dst, row, lo=0, hi=KD // 2):
                    for kk in range(lo, hi):
                        act.wait_ge(s["tp_done"], p.q + 1)
                        src = bank(6 + p.q % 2).rearrange("p (k t) -> p k t", k=2)
                        for k in range(2):
                            ins = copy(dst[:, 2 * kk + k, :], src[:, k, :], cT[:, row + 2 * kk + k:row + 2 * kk + k + 1])
                        ins.then_inc(s["hi_evac"], 1)
                        p.q += 1

                def norm_in(dst, row, ue):
                    split_to(ue + 1)
                    evac_norm(dst, row, 0, 2)
                    split_to(ue + 2)
                    evac_norm(dst, row, 2, 4)

                def chunk_in(ue):
                    split_to(ue + 2)
                    act.wait_ge(s["unit_used"], ue + 1)

                mem_junk = Bl[:, :, :].rearrange("p a b -> p (a b)").rearrange("p (t d) -> p t d", t=NT)
                for t in range(NT):
                    act.wait_ge(s["mem_t1_loaded" if t else "mem_loaded"], 16)
                    for c in range(2):
                        sumsq(xm, mem_junk, c, (t,))
                p.n += 1
                act.wait_ge(s["consts_done"], 1)
                copy(cT[:], bank(7)[:, 0:ROWS]).then_inc(s["consts_used"], 1)
                act.wait_ge(s["consts_used"], 1)
                evac_norm(Mh, G_MEM, 0, 2)
                split_to(0)
                evac_norm(Mh, G_MEM, 2, 4)
                split_to(1)
                act.wait_ge(s["x_loaded"], 16)
                for c in range(2):
                    sumsq(x, xn, c)
                p.n += 1
                ue = 1
                for c in range(2):
                    if c:
                        norm_in(Ah, G_MIX, ue)
                    chunk_in(ue)
                    copy(kT[:, 4 * c:4 * c + 4, :], tiles_of(p.c)).then_inc(pair_free[p.c % 3], 1)
                    p.c += 1
                    ue += 2
                chunk_in(ue)
                copy(cols(vv, 0), pair(p.c).rearrange("p (t n) -> p t n", t=NT)).then_inc(pair_free[p.c % 3], 1)
                p.c += 1
                for l in range(DEPTH):
                    ue += 2
                    chunk_in(ue)
                    copy(up[:, :, PAD:], tiles_of(p.c)).then_inc(pair_free[p.c % 3], 1)
                    p.c += 1
                    ue += 2
                    chunk_in(ue)
                    copy(cg[:, :, :], tiles_of(p.c)).then_inc(pair_free[p.c % 3], 1)
                    p.c += 1
                    ue += 2
                    chunk_in(ue)
                    copy(bg[:, :, :], tiles_of(p.c)).then_inc(pair_free[p.c % 3], 1)
                    p.c += 2
                    ue += 2
                    for i in range(4):
                        ue += 2
                        chunk_in(ue)
                        act.activation(gT[:, 4 * i:4 * i + 4, :], tiles_of(p.c), ACT.Sigmoid
                                       ).then_inc(pair_free[p.c % 3], 1)
                        p.c += 1
                        if i == 1:
                            act.wait_ge(s["conv_ready"], l + 1)
                            copy(Bh[:, 4:8, :], cg[:, :, :]).then_inc(s["hi_evac"], 1)
                            split_to(ue + 3)
                            act.wait_ge(s["group_done"], l + 1)
                            for g in range(NG):
                                r = R_SCALE + l * NG + g
                                ins = copy(Bh[:, g, :], tiles_of(p.c)[:, g, :], cT[:, r:r + 1])
                            ins.then_inc(s["hi_evac"], 1)
                            p.c += 1
                    ue += 2
                    p.c += 2
                    for c in range(2):
                        split_to(ue + 3 + c)
                        act.wait_ge(s["merged_f"], 2 * l + c + 1)
                        copy(Ah[:, 4 * c:4 * c + 4, :], gT[:, 4 * c:4 * c + 4, :]).then_inc(s["hi_evac"], 1)
                        p.c += 1
                    ue += 2
                    ue += 2
                    split_to(ue + 2)
                    ue += 2
                    split_to(ue + 2)
                    p.c += 2
                    x_sumsq()
                    ue += 2
                    norm_in(Ah, G_XATTN + l * KD, ue)
                    chunk_in(ue)
                    copy(cols(vv, 1), pair(p.c).rearrange("p (t n) -> p t n", t=NT)).then_inc(pair_free[p.c % 3], 1)
                    p.c += 1
                    for c in range(2):
                        ue += 2
                        chunk_in(ue)
                        copy(qT[:, 4 * c:4 * c + 4, :], tiles_of(p.c), float(HD) ** -0.5
                             ).then_inc(pair_free[p.c % 3], 1)
                        p.c += 1
                        if l == 0 and c == 0:
                            act.wait_ge(s["mem_loaded"], 32)
                            for n in range(2):
                                sumsq(xm, mem_junk, n)
                            p.n += 1
                    def probs_t(h):
                        act.wait_ge(s["tp_done"], p.q + 1)
                        copy(pT[:, h, :, :], bank(6 + p.q % 2).rearrange("p (m t) -> p m t", m=NT)
                             ).then_inc(tp_free[p.q % 2], 1)
                        p.q += 1

                    for h in range(NH):
                        act.wait_ge(s["max_ready"], NH * l + h + 1)
                        src = bank(2 * ((p.c + h // 2) % 3) + h % 2).rearrange("p (t m) -> p t m", t=NT)
                        for t in range(NT):
                            ins = act.activation(pr[:, h, t, :], src[:, t, :], ACT.Exp, bias=nmx[:, l, h, t:t + 1],
                                                 accum_out=sm[:, l, h, t:t + 1])
                        ins.then_inc(s["exp_done"], 1)
                        if h == 2:
                            probs_t(0)
                    p.c += 2

                    def o_hi(h):
                        act.wait_ge(s["o_done"], NH * l + h + 1)
                        src = bank(2 * ((p.c + h // 2) % 3) + h % 2).rearrange("p (d t) -> p d t", d=2)
                        copy(Ah[:, 2 * h:2 * h + 2, :], src).then_inc(s["hi_evac"], 1)

                    for h in range(1, NH):
                        probs_t(h)
                        o_hi(h - 1)
                    o_hi(NH - 1)
                    p.c += 2
                    ue += 2
                    split_to(ue + 2)
                    p.c += 2
                    if l == 0:
                        evac_norm(Mh, G_MEM + KD, 0, 2)
                        split_to(ue + 3)
                        evac_norm(Mh, G_MEM + KD, 2, 4)
                    ue += 2
                    split_to(ue + 2)
                    if l == DEPTH - 1:
                        for i in range(AHEAD - 1):
                            expert_hi(i, 0)
                    x_sumsq()
                    if l == 0:
                        for c in range(2):
                            ue += 2
                            if c:
                                norm_in(Ah, G_FFN, ue)
                            chunk_in(ue)
                            copy(kT[:, 4 * c:4 * c + 4, :], tiles_of(p.c)).then_inc(pair_free[p.c % 3], 1)
                            p.c += 1
                        for f in range(2):
                            for i, (c0, n) in enumerate(FCH):
                                nf = n // P
                                ue += 2
                                chunk_in(ue)
                                act.activation(st2[i % 2][:, 0:nf, :], tiles_of(p.c, nf), ACT.Silu
                                               ).then_inc(pair_free[p.c % 3], 1)
                                p.c += 2
                                ue += 2
                                split_to(ue + 2)
                                act.wait_ge(pair_free[(p.c - 1) % 3], u_free(p.c - 1))
                                copy(Fh[:, 4 * i:4 * i + nf, :], st2[i % 2][:, 0:nf, :]).then_inc(s["hi_evac"], 1)
                            for c in range(2):
                                ue += 3
                                split_to(ue + 2)
                                p.c += 1
                            if f == 0:
                                x_sumsq.n += 1
                        x_sumsq()
                        ue += 2
                        norm_in(Ah, G_MIX + KD, ue)
                        chunk_in(ue)
                        copy(cols(vv, 0), pair(p.c).rearrange("p (t n) -> p t n", t=NT)).then_inc(pair_free[p.c % 3], 1)
                        p.c += 1
                    else:
                        act.wait_ge(s["wrt_loaded"], 16)
                        act.wait_ge(s["merged_ready"], 2 * DEPTH)
                        copy(wr2[:, :, 0:NE], wrt[:]).then_inc(s["wrh_ready"], 1)
                        evac_norm(Ah, G_FFN + KD)

                def gathered_hi(v):
                    for b in range(2):
                        act.wait_ge(s["g_done"], 2 * v + (b + 1))
                        copy(heh[:, 4 * b:4 * b + 4, :], bank(2 + b).rearrange("p (k c) -> p k c", c=P)
                             ).then_inc(s["hehi_ready"], 1)

                def act_hi(j, v):
                    act.wait_ge(s["t_done"], v * NJ + (j + 1))
                    copy(aTh[j % 2], bank(6).rearrange("p (f c) -> p f c", c=P)).then_inc(s["acthi_ready"], 1)

                def visit(v, more):
                    act.activation(first_silu[:], mhalf[:, 0:1], ACT.Silu)
                    for i in range(AHEAD, BODY):
                        expert_hi(i, v)
                        if i == AHEAD:
                            act.wait_ge(s["unit_used"], v * BODY + U0)
                            copy(yh, ps[:, 4:6, :].rearrange("p a b -> p (a b)"), gc[:, 0:1]).then_inc(s["yhi_ready"], 1)
                        for j in range(NJ):
                            if i == gu_start(j) + 3:
                                act.wait_ge(s["unit_used"], v * BODY + (U0 + gu_start(j) + 2))
                                if j:
                                    act.wait_ge(s["act_ready"], v * NJ + j)
                                act.activation(silu_t[:], bank(2 * (j % 2)), ACT.Silu).then_inc(s["silu_ready"], 1)
                                if j:
                                    act_hi(j - 1, v)
                    act_hi(NJ - 1, v)
                    if more:
                        expert_hi(BODY, v)
                        gathered_hi(v + 1)
                        for i in range(1, AHEAD):
                            expert_hi(BODY + i, v)

                expert_hi(AHEAD - 1, 0)
                act.wait_ge(s["logits_done"], 1)
                copy(lgT[:], bank(0)[0:2 * NE, 0:SEQ]).then_inc(s["lgT_ready"], 1)
                act.wait_ge(s["sel_ready"], 1)
                act.activation(rc[3][:], rc[2][:], ACT.Exp).then_inc(s["exp2_done"], 1)
                gathered_hi(0)
                act.wait_ge(s["zero_done"], 1)
                act.wait_ge(s["visits_ready"], 1)
                last_visit = act.value_load(nvis[0:1, 1:2], min_val=NE - 1, max_val=2 * NE - 1)
                with act.Fori(0, last_visit) as v:
                    visit(v, True)
                visit(last_visit, False)

            @block.vector
            def _(dve):
                p = At()
                chain = [0]

                def link(ins):
                    chain[0] += 1
                    ins.then_inc(s["dve_chain"], 1)
                    dve.wait_ge(s["dve_chain"], chain[0])

                def split_to(u):
                    while p.u <= min(u, U0 - 1):
                        n = p.u
                        dve.wait_ge(s["hi_ready"], n + 1)
                        size = units[n][2] * units[n][4]
                        dve.tensor_tensor(wlo[n % SPL][:, 0:size], raw[n % RAW][:, 0:size],
                                          whi[n % SPL][:, 0:size].bitcast(F32), ALU.subtract).then_inc(s["lo_ready"], 1)
                        p.u += 1

                def minus(dst, src, hi):
                    return dve.tensor_tensor(dst, src, hi.bitcast(F32), ALU.subtract)

                def hi_wait():
                    p.h += 1
                    dve.wait_ge(s["hi_evac"], p.h)

                def normalize(src, dst):
                    dve.wait_ge(s["rstd_ready"], p.n + 1)
                    for t in range(NT):
                        dve.tensor_scalar(dst[:, t, :], src[:, t, :], rstd[:, p.n, t:t + 1], None, ALU.mult
                                          ).then_inc(s["xn_ready"], 1)
                    p.n += 1

                def evac_norm(dst, hi, row, k0=0, k1=KD // 2):
                    for kk in range(k0, k1):
                        hi_wait()
                        src = bank(6 + p.q % 2).rearrange("p (k t) -> p k t", k=2)
                        for k in range(2):
                            n = 2 * kk + k
                            ins = dve.scalar_tensor_tensor(out=dst[:, n, :], in0=src[:, k, :],
                                                           scalar=cT[:, row + n:row + n + 1],
                                                           in1=hi[:, n, :].bitcast(F32), op0=ALU.mult, op1=ALU.subtract)
                        ins.then_inc(tp_free[p.q % 2], 1)
                        p.q += 1

                def norm_in(dst, hi, row, ue):
                    split_to(ue + 1)
                    evac_norm(dst, hi, row, 0, 2)
                    split_to(ue + 2)
                    evac_norm(dst, hi, row, 2, 4)
                    p.c += 1

                def expert_lo(i, v):
                    u = U0 + i
                    dve.wait_ge(s["hi_ready"], v * BODY + (u + 1))
                    minus(wlo[u % SPL][:], moe_raw(i), whi[u % SPL][:]).then_inc(s["lo_ready"], 1)

                def x_add(ue):
                    split_to(ue + 2)
                    dve.wait_ge(s["unit_used"], ue + 1)
                    c = x_add.n % 2
                    x_add.n += 1
                    src = pair(p.c).rearrange("p (t n) -> p t n", t=NT)
                    if c == 0:
                        dve.tensor_tensor(cols(x, c), cols(x, c), src, ALU.add).then_inc(pair_free[p.c % 3], 1)
                    else:
                        for t in range(NT):
                            xs = x[:, t, C:]
                            dve.tensor_tensor(xs, xs, src[:, t, :], ALU.add
                                              ).then_inc(pair_free[p.c % 3] if t else s["x_half"], 1)
                    p.c += 1
                x_add.n = 0

                def free(c):
                    return pair_free[c % 3]

                dve.wait_ge(s["setup_done"], 1)
                link(dve.reciprocal(inv[:], inv[:]))
                normalize(xm, xm)
                dve.wait_ge(s["consts_used"], 1)
                evac_norm(Ml, Mh, G_MEM, 0, 2)
                split_to(0)
                evac_norm(Ml, Mh, G_MEM, 2, 4)
                split_to(1)
                normalize(x, xn)
                p.c += 1
                ue = 3
                norm_in(Al, Ah, G_MIX, ue)
                ue += 2
                split_to(ue + 2)
                p.c += 1
                for l in range(DEPTH):
                    ue += 2
                    split_to(ue + 2)
                    dve.wait_ge(pair_free[p.c % 3], u_free(p.c))
                    dve.wait_ge(s["pads_ready"], l + 1)
                    E = PAD + SEQ
                    link(dve.tensor_tensor(s1[:, :, 1:], up[:, :, 1:], up[:, :, 0:E - 1], ALU.add))
                    link(dve.tensor_tensor(s2[:, 1:, 3:], s1[:, 1:, 3:], s1[:, 1:, 1:E - 2], ALU.add))
                    ue += 2
                    split_to(ue + 2)
                    link(dve.tensor_tensor(s1[:, 2:, 7:], s2[:, 2:, 7:], s2[:, 2:, 3:E - 4], ALU.add))
                    link(dve.tensor_tensor(s2[:, 3:, PAD:], s1[:, 3:, PAD:], s1[:, 3:, PAD - 8:E - 8], ALU.add))
                    for g, w in enumerate(WINDOWS):
                        src = (s1, s2)[g % 2]
                        last = dve.scalar_tensor_tensor(out=pp[:, g, :], in0=src[:, g, PAD:], scalar=1.0 / w,
                                                        in1=up[:, g, PAD:], op0=ALU.mult, op1=ALU.subtract)
                    link(last)
                    ue += 2
                    split_to(ue + 2)
                    for g in range(NG):
                        src = (s1, s2)[g % 2]
                        last = dve.tensor_tensor(pp[:, g, 0:PAD], src[:, g, PAD:2 * PAD], inv[:, g, :], ALU.mult)
                    link(last)
                    dve.tensor_tensor(pp[:, :, 0:PAD], pp[:, :, 0:PAD], up[:, :, PAD:2 * PAD], ALU.subtract
                                      ).then_inc(s["pooled_ready"], 1)
                    p.c += 3
                    ue += 2
                    split_to(ue + 2)
                    dve.wait_ge(s["unit_used"], ue + 1)
                    dve.wait_ge(pair_free[(p.c - 2) % 3], u_free(p.c - 2))
                    dve.wait_ge(pair_free[(p.c - 1) % 3], u_free(p.c - 1))
                    ins = dve.tensor_tensor(zc[:, :, CK - 1:], cg[:, :, :], tiles_of(p.c), ALU.mult)
                    ins.then_inc(free(p.c), 1)
                    dve.wait_ge(free(p.c), u_free(p.c))
                    p.c += 1
                    for j in range(CK):
                        for g in range(NG):
                            r = R_CONV + (l * CK + j) * NG + g
                            w = cT[:, r:r + 1]
                            if j == 0:
                                last = dve.tensor_scalar(cg[:, g, :], zc[:, g, 0:SEQ], w, None, ALU.mult)
                            else:
                                last = dve.scalar_tensor_tensor(out=cg[:, g, :], in0=zc[:, g, j:j + SEQ], scalar=w,
                                                                in1=cg[:, g, :], op0=ALU.mult, op1=ALU.add)
                        link(last)
                    dve.tensor_tensor(cg[:], cg[:], bg[:], ALU.mult).then_inc(s["conv_ready"], 1)
                    ue += 4
                    split_to(ue + 2)
                    hi_wait()
                    minus(Bl[:, 4:8, :], cg[:], Bh[:, 4:8, :]).then_inc(s["yc_ready"], 1)
                    p.c += 2
                    split_to(ue + 3)
                    hi_wait()
                    for g in range(NG):
                        r = R_SCALE + l * NG + g
                        ins = dve.scalar_tensor_tensor(out=Bl[:, g, :], in0=tiles_of(p.c)[:, g, :], scalar=cT[:, r:r + 1],
                                                       in1=Bh[:, g, :].bitcast(F32), op0=ALU.mult, op1=ALU.subtract)
                    ins.then_inc(free(p.c), 1)
                    p.c += 1
                    ue += 4
                    split_to(ue + 2)
                    p.c += 2
                    for c in range(4):
                        ue += 1
                        split_to(ue + (2 if c < 3 else 1))
                        dve.wait_ge(s["unit_used"], ue + 1)
                        if c == 0:
                            dve.wait_ge(free(p.c - 1), u_free(p.c - 1))
                        g = gT[:, 4 * c:4 * c + 4, :]
                        ins = dve.tensor_tensor(g, g, tiles_of(p.c), ALU.mult)
                        ins.then_inc(free(p.c), 1)
                        p.c += 1
                        if c >= 2:
                            dve.wait_ge(free(p.c - 1), u_free(p.c - 1))
                            m = gT[:, 4 * (c - 2):4 * (c - 2) + 4, :]
                            dve.tensor_tensor(m, m, g, ALU.add).then_inc(s["merged_f"], 1)
                            split_to(ue + 2)
                            hi_wait()
                            minus(Al[:, 4 * (c - 2):4 * (c - 2) + 4, :], m, Ah[:, 4 * (c - 2):4 * (c - 2) + 4, :]
                                  ).then_inc(s["merged_ready"], 1)
                    for c in range(2):
                        ue += 2
                        x_add(ue)
                    normalize(x, xn)
                    ue += 2
                    norm_in(Al, Ah, G_XATTN + l * KD, ue)
                    ue += 4
                    split_to(ue + 2)
                    p.c += 2
                    for h in range(NH + 1):
                        if h < NH:
                            dve.wait_ge(s["scores_done"], NH * l + h + 1)
                            src = bank(2 * ((p.c + h // 2) % 3) + h % 2).rearrange("p (t m) -> p t m", t=NT)
                            link(dve.tensor_reduce(mx[:, l, h, :], src, AX_X, ALU.max))
                            dve.tensor_scalar(nmx[:, l, h, :], mx[:, l, h, :], -1.0, None, ALU.mult
                                              ).then_inc(s["max_ready"], 1)
                        if h == 0:
                            continue
                        h -= 1
                        dve.wait_ge(s["exp_done"], NH * l + h + 1)
                        link(dve.reciprocal(rs[:, l, h, :], sm[:, l, h, :]))
                        for t in range(NT):
                            ins = dve.tensor_scalar(pr[:, h, t, :], pr[:, h, t, :], rs[:, l, h, t:t + 1], None, ALU.mult)
                            if t == 0 and h % 2:
                                ins.then_inc(pair_free[(p.c + h // 2) % 3], 1)
                        ins.then_inc(s["probs_ready"], 1)
                    p.c += 2
                    p.q += NH
                    for h in range(NH):
                        hi_wait()
                        src = bank(2 * ((p.c + h // 2) % 3) + h % 2).rearrange("p (d t) -> p d t", d=2)
                        ins = minus(Al[:, 2 * h:2 * h + 2, :], src, Ah[:, 2 * h:2 * h + 2, :])
                        ins.then_inc(pair_free[(p.c + h // 2) % 3] if h % 2 else s["o_ready"], 1)
                    p.c += 2
                    ue += 2
                    if l == 0:
                        split_to(ue + 2)
                        normalize(xm, xm)
                        x_add(ue)
                        evac_norm(Ml, Mh, G_MEM + KD, 0, 2)
                        split_to(ue + 3)
                        evac_norm(Ml, Mh, G_MEM + KD, 2, 4)
                    else:
                        x_add(ue)
                    ue += 2
                    if l == DEPTH - 1:
                        for i in range(AHEAD - 1):
                            expert_lo(i, 0)
                    x_add(ue)
                    normalize(x, xn)
                    if l == 0:
                        ue += 2
                        split_to(ue + 2)
                        p.c += 1
                        ue += 2
                        norm_in(Al, Ah, G_FFN, ue)
                        for f in range(2):
                            for i, (c0, n) in enumerate(FCH):
                                nf = n // P
                                ue += 2
                                split_to(ue + 2)
                                ue += 2
                                split_to(ue + 2)
                                dve.wait_ge(free(p.c), u_free(p.c))
                                p.c += 1
                                dve.wait_ge(s["unit_used"], ue + 1)
                                t_ = st2[i % 2][:, 0:nf, :]
                                ins = dve.tensor_tensor(t_, t_, tiles_of(p.c, nf), ALU.mult)
                                ins.then_inc(free(p.c), 1)
                                hi_wait()
                                minus(Fl[:, 4 * i:4 * i + nf, :], t_, Fh[:, 4 * i:4 * i + nf, :]).then_inc(s["ff_ready"], 1)
                                p.c += 1
                            for c in range(2):
                                ue += 3
                                x_add(ue)
                        normalize(x, xn)
                        ue += 2
                        norm_in(Al, Ah, G_MIX + KD, ue)
                dve.wait_ge(s["setup_done"], 2)
                dve.wait_ge(s["wrh_ready"], 1)
                dve.tensor_tensor(fold[:], ident[0:2 * NE, 0:NE], ident[0:2 * NE, NE:2 * NE], ALU.add)
                minus(wr2[:, :, NE:], wrt[:], wr2[:, :, 0:NE]).then_inc(s["wrl_ready"], 1)
                for c in range(p.c - 3, p.c):
                    dve.wait_ge(free(c), u_free(c))
                dve.memset(ps[:, 4:6, :], 0.0).then_inc(s["zero_done"], 1)
                evac_norm(Al, Ah, G_FFN + KD)
                expert_lo(AHEAD - 1, 0)
                dve.wait_ge(s["lg_done"], 1)
                lg = bank(1)[:, 0:NT * NE].rearrange("p (t e) -> p t e", t=NT)

                def first_max(src, top, hot, tmp, r):
                    link(dve.tensor_reduce(top[:], src, AX_X, ALU.max))
                    for t in range(NT):
                        last = dve.scalar_tensor_tensor(out=tmp[:, t, :], in0=src[:, t, :], scalar=top[:, t:t + 1],
                                                        in1=rev[:, t, :], op0=ALU.is_equal, op1=ALU.mult)
                    link(last)
                    link(dve.tensor_reduce(r[:], tmp[:], AX_X, ALU.max))
                    for t in range(NT):
                        last = dve.tensor_scalar(hot[:, t, :], rev[:, t, :], r[:, t:t + 1], None, ALU.is_equal)
                    link(last)

                first_max(lg, rc[0], rt[0], rt[1], rc[4])
                link(dve.scalar_tensor_tensor(out=rt[2][:], in0=rt[0][:], scalar=-BIG, in1=lg, op0=ALU.mult, op1=ALU.add))
                first_max(rt[2][:], rc[1], rt[3], rt[1], rc[5])
                dve.tensor_tensor(rt[4][:], rt[0][:], rt[3][:], ALU.add).then_inc(s["hot_ready"], 1)
                dve.tensor_tensor(rc[2][:], rc[1][:], rc[0][:], ALU.subtract).then_inc(s["sel_ready"], 1)

                def select(col):
                    for t in range(NT):
                        ins = dve.tensor_scalar(S[:, t, :], iota[:], posm[:, t, col], None, ALU.is_equal)
                    ins.then_inc(s["s_ready"], 1)

                def gathered_lo(v):
                    for b in range(2):
                        dve.wait_ge(s["hehi_ready"], 2 * v + (b + 1))
                        minus(hel[:, 4 * b:4 * b + 4, :], bank(2 + b).rearrange("p (k c) -> p k c", c=P),
                              heh[:, 4 * b:4 * b + 4, :]).then_inc(s["he_ready"], 1)

                def act_lo(j, v):
                    dve.wait_ge(s["acthi_ready"], v * NJ + (j + 1))
                    minus(aTl[j % 2], bank(6).rearrange("p (f c) -> p f c", c=P), aTh[j % 2]).then_inc(s["actT_ready"], 1)

                def add_piece(n, v):
                    dve.wait_ge(s["sc_done"], v * 4 + (n + 1))
                    t, c = n // 2, n % 2
                    xs = x[:, t, c * C:(c + 1) * C]
                    dve.tensor_tensor(xs, xs, bank(6 if n == 0 else 7), ALU.add).then_inc(s["xadd_done"], 1)

                def visit(v, more):
                    for i in range(AHEAD, BODY):
                        expert_lo(i, v)
                        if i == AHEAD:
                            dve.wait_ge(s["yhi_ready"], v + 1)
                            dve.scalar_tensor_tensor(out=yl, in0=ps[:, 4:6, :].rearrange("p a b -> p (a b)"),
                                                     scalar=gc[:, 0:1], in1=yh.bitcast(F32), op0=ALU.mult,
                                                     op1=ALU.subtract).then_inc(s["y_ready"], 1)
                        for j in range(NJ):
                            if j and i == gu_start(j) + 3:
                                act_lo(j - 1, v)
                            if i == gu_start(j) + 5:
                                dve.wait_ge(s["unit_used"], v * BODY + (U0 + gu_start(j) + 4))
                                dve.wait_ge(s["silu_ready"], v * NJ + (j + 1))
                                dve.tensor_tensor(act_t[:], silu_t[:], bank(2 * (j % 2) + 1), ALU.mult
                                                  ).then_inc(s["act_ready"], 1)
                        if i == gu_start(0) + 5:
                            add_piece(0, v)
                        if i == gu_start(0) + 6:
                            add_piece(1, v)
                        if i == gu_start(1) + 5:
                            add_piece(2, v)
                        if i == gu_start(2) + 5:
                            add_piece(3, v)
                        if i == gu_start(3) + 5:
                            dve.wait_ge(s["ts_done"], v + 1)
                            dve.tensor_copy(ST[:], bank(7)[:, 0:SEQ])
                            dve.tensor_copy(gc[:], bank(7)[:, SEQ:SEQ + 1]).then_inc(s["st_ready"], 1)
                            select(bass.ds(v + 1, 1))
                    act_lo(NJ - 1, v)
                    if more:
                        expert_lo(BODY, v)
                        gathered_lo(v + 1)
                        for i in range(1, AHEAD):
                            expert_lo(BODY + i, v)

                dve.wait_ge(s["rank_done"], 1)
                rk = bank(0)[:, 0:NT * NE].rearrange("p (t e) -> p t e", t=NT)
                link(dve.scalar_tensor_tensor(out=posm[:, :, 0:NE], in0=rk, scalar=1.0, in1=rt[4][:], op0=ALU.add,
                                              op1=ALU.mult))
                select(slice(0, 1))
                dve.tensor_scalar(posm[:, :, NE:2 * NE], posm[:, :, 0:NE], -float(P), None, ALU.add)
                dve.wait_ge(s["count_done"], 1)
                link(dve.tensor_copy(rt[1][:], bank(1)[:, 0:NT * NE].rearrange("p (t e) -> p t e", t=NT)))
                link(dve.tensor_tensor(rt[2][:, 0, :], rt[1][:, 0, :], rt[1][:, 1, :], ALU.add))
                link(dve.tensor_reduce(cnt[:, 0:1], rt[2][:, 0, :], AX_X, ALU.max))
                link(dve.tensor_scalar(cnt[:, 1:2], cnt[:, 0:1], float(P), float(NE), ALU.is_gt, ALU.mult))
                dve.tensor_scalar(nvis[:, 0:1], cnt[:, 1:2], float(NE), None, ALU.add)
                dve.tensor_scalar(nvis[:, 1:2], cnt[:, 1:2], float(NE - 1), None, ALU.add).then_inc(s["visits_ready"], 1)
                gathered_lo(0)
                dve.wait_ge(s["exp2_done"], 1)
                link(dve.tensor_scalar(rc[4][:], rc[3][:], 1.0, None, ALU.add))
                link(dve.reciprocal(rc[5][:], rc[4][:]))
                link(dve.tensor_tensor(rc[6][:], rc[3][:], rc[5][:], ALU.mult))
                for t in range(NT):
                    last = dve.tensor_scalar(rt[5][:, t, :], rt[3][:, t, :], rc[6][:, t:t + 1], None, ALU.mult)
                link(last)
                for t in range(NT):
                    last = dve.scalar_tensor_tensor(out=gate2[:, t, 0:NE], in0=rt[0][:, t, :], scalar=rc[5][:, t:t + 1],
                                                    in1=rt[5][:, t, :], op0=ALU.mult, op1=ALU.add)
                link(last)
                dve.tensor_copy(gate2[:, :, NE:2 * NE], gate2[:, :, 0:NE]).then_inc(s["gate2_ready"], 1)
                dve.wait_ge(s["visits_ready"], 1)
                last_visit = dve.value_load(nvis[0:1, 1:2], min_val=NE - 1, max_val=2 * NE - 1)
                with dve.Fori(0, last_visit) as v:
                    visit(v, True)
                visit(last_visit, False)

            @block.tensor
            def _(pe):
                p = At()
                PASSES = ((0, 0), (0, 1), (1, 0))

                def take_pair():
                    if p.c >= 3:
                        pe.wait_ge(pair_free[p.c % 3], p.c // 3)

                def parts(u):
                    return unit_view(whi[u % SPL], u), unit_view(wlo[u % SPL], u)

                def chunk_t(n_units, xs, ready, between=None):
                    take_pair()
                    o = tiles_of(p.c)
                    for j in range(n_units):
                        _, k0, nk, _, nn = units[p.u]
                        w = parts(p.u)
                        pe.wait_ge(s["lo_ready"], p.u + 1)
                        for k in range(nk):
                            ready(k0 + k)
                            for d in range(nn // P):
                                for n, (wi, xi) in enumerate(PASSES):
                                    first = j == 0 and k == 0 and n == 0
                                    last = j == n_units - 1 and k == nk - 1 and n == 2
                                    ins = pe.matmul(o[:, d, :], w[wi][:, k, d * P:(d + 1) * P], xs[xi][:, k0 + k, :],
                                                    start=first and d % 2 == 0, stop=last, skip_group_check=True)
                        ins.then_inc(s["unit_used"], 1)
                        p.u += 1
                        if between and j == 0:
                            between()
                    p.c += 1

                def chunk_n(n_units, xs, ready, between=None):
                    take_pair()
                    o = pair(p.c).rearrange("p (t n) -> p t n", t=NT)
                    for j in range(n_units):
                        _, k0, nk, _, nn = units[p.u]
                        w = parts(p.u)
                        pe.wait_ge(s["lo_ready"], p.u + 1)
                        for k in range(nk):
                            ready(k0 + k)
                            for t in range(NT):
                                for n, (wi, xi) in enumerate(PASSES):
                                    ins = pe.matmul(o[:, t, 0:nn], xs[xi][:, k0 + k, t * P:(t + 1) * P], w[wi][:, k, :],
                                                    start=j == 0 and k == 0 and n == 0,
                                                    stop=j == n_units - 1 and k == nk - 1 and n == 2)
                        ins.then_inc(s["unit_used"], 1)
                        p.u += 1
                        if between and j == 0:
                            between()
                    p.c += 1

                def once(sem, value_of):
                    seen = [0]

                    def ready(k):
                        v = value_of(k)
                        if v > seen[0]:
                            pe.wait_ge(sem, v)
                            seen[0] = v
                    return ready

                def already(k):
                    return None

                def take_bank():
                    if tpn[p.q % 2]:
                        pe.wait_ge(tp_free[p.q % 2], tpn[p.q % 2])
                    tpn[p.q % 2] += 1
                tpn = [0, 0]

                def transposes(src, lo, hi):
                    for kk in range(lo, hi):
                        take_bank()
                        b = bank(6 + p.q % 2).rearrange("p (k t) -> p k t", k=2)
                        for t in range(NT):
                            if kk == lo:
                                pe.wait_ge(s["xn_ready"], 2 * p.n + t + 1)
                            for k in range(2):
                                n = 2 * kk + k
                                ins = pe.transpose(b[:, k, t * P:(t + 1) * P], src[:, t, n * P:(n + 1) * P], ident[:])
                        ins.then_inc(s["tp_done"], 1)
                        p.q += 1
                    if hi == KD // 2:
                        p.n += 1

                def normed(q0):
                    seen = set()

                    def ready(k):
                        q = q0 + k // 2
                        if q not in seen:
                            seen.add(q)
                            pe.wait_ge(tp_free[q % 2], q // 2 + 1)
                    return ready

                def keep_clock(n):
                    take_pair()
                    for _ in range(n):
                        pe.matmul(pair(p.c)[:, 0:P], ident[:], ident[:], start=True, stop=True)

                MEM, XA, XB, FF = (Mh, Ml), (Ah, Al), (Bh, Bl), (Fh, Fl)
                pe.wait_ge(s["setup_done"], 1)
                keep_clock(10)
                pe.wait_ge(s["const_loaded"], 16 * 6)
                pe.transpose(bank(7)[:, 0:P], rows[:], ident[:]).then_inc(s["consts_done"], 1)
                keep_clock(8)
                pe.wait_ge(s["consts_used"], 1)
                q_mem = p.q
                transposes(xm, 0, KD // 2)
                ready = normed(q_mem)
                chunk_t(2, MEM, ready)
                q_h = p.q
                chunk_t(2, MEM, already, lambda: transposes(xn, 0, 2))
                transposes(xn, 2, 4)
                chunk_n(2, MEM, already)
                for l in range(DEPTH):
                    ready = normed(q_h)
                    for c in range(6):
                        chunk_t(2, XA, ready)
                    take_pair()
                    pe.wait_ge(s["pooled_ready"], l + 1)
                    pe.wait_ge(s["wpg_loaded"], 16 * (l + 1))
                    for g in range(NG):
                        ins = pe.matmul(tiles_of(p.c)[:, g, :], wpg[:, g, :], pp[:, g, :], start=True, stop=True)
                    ins.then_inc(s["group_done"], 1)
                    c_group = p.c
                    p.c += 1
                    for c in range(2):
                        chunk_t(2, XA, already)
                    pe.wait_ge(pair_free[c_group % 3], c_group // 3 + 1)
                    for c in range(2):
                        chunk_t(1, XB, already)
                    pe.wait_ge(s["yc_ready"], l + 1)
                    for c in range(2):
                        chunk_t(1, (Bh[:, 4:8, :], Bl[:, 4:8, :]), already)
                    ready = once(s["merged_ready"], lambda k: 2 * l + k // 4 + 1)
                    for c in range(2):
                        chunk_n(2, XA, ready)
                    q_h = p.q
                    chunk_n(2, MEM, already, lambda: transposes(xn, 0, 2))
                    transposes(xn, 2, KD // 2)
                    ready = normed(q_h)
                    for c in range(2):
                        chunk_t(2, XA, ready)
                    def probs_t(h):
                        pe.wait_ge(s["probs_ready"], NH * l + h + 1)
                        take_bank()
                        b = bank(6 + p.q % 2).rearrange("p (m t) -> p m t", m=NT)
                        for m in range(NT):
                            for t in range(NT):
                                ins = pe.transpose(b[:, m, t * P:(t + 1) * P], pr[:, h, t, m * P:(m + 1) * P], ident[:])
                        ins.then_inc(s["tp_done"], 1)
                        p.q += 1

                    q_p = p.q
                    c_q = p.c - 2
                    for h in range(NH):
                        if h % 2 == 0:
                            c = c_q + h // 2
                            pe.wait_ge(pair_free[c % 3], c // 3 + 1)
                            take_pair()
                        b = bank(2 * (p.c % 3) + h % 2)
                        for t in range(NT):
                            for d in range(2):
                                ins = pe.matmul(b[:, t * SEQ:(t + 1) * SEQ], qT[:, 2 * h + d, t * P:(t + 1) * P],
                                                kT[:, 2 * h + d, :], start=d == 0, stop=d == 1)
                        ins.then_inc(s["scores_done"], 1)
                        if h % 2:
                            p.c += 1
                        if h == 2:
                            probs_t(0)

                    def head_out(h):
                        if h % 2 == 0:
                            take_pair()
                        q = q_p + h
                        pe.wait_ge(tp_free[q % 2], q // 2 + 1)
                        b = bank(2 * (p.c % 3) + h % 2)
                        for d in range(2):
                            for m in range(NT):
                                ins = pe.matmul(b[:, d * SEQ:(d + 1) * SEQ], vv[:, m, h * HD + d * P:h * HD + (d + 1) * P],
                                                pT[:, h, m, :], start=m == 0, stop=m == NT - 1)
                        ins.then_inc(s["o_done"], 1)
                        if h % 2:
                            p.c += 1

                    c_o = p.c
                    for h in range(1, NH):
                        probs_t(h)
                        head_out(h - 1)
                    head_out(NH - 1)
                    seen = set()

                    def ready(k):
                        h = k // 2
                        if h not in seen:
                            seen.add(h)
                            c = c_o + h // 2
                            if h % 2:
                                pe.wait_ge(pair_free[c % 3], u_free(c))
                            else:
                                pe.wait_ge(s["o_ready"], NH // 2 * l + h // 2 + 1)
                    chunk_n(2, XA, ready)
                    q_mem = p.q
                    if l == 0:
                        transposes(xm, 0, 2)
                        chunk_n(2, XA, already, lambda: transposes(xm, 2, 4))
                        ready = normed(q_mem)
                        chunk_t(2, MEM, ready)
                        q_h = p.q
                        chunk_t(2, MEM, already, lambda: transposes(xn, 0, 2))
                        transposes(xn, 2, 4)
                        ready = normed(q_h)
                        for f in range(2):
                            for i in range(len(FCH)):
                                chunk_t(2, XA, ready)
                                chunk_t(2, XA, already)
                            ready = already
                            r = once(s["ff_ready"], lambda k: 3 * f + k // 4 + 1)
                            for c in range(2):
                                chunk_n(3, FF, r)
                        q_h = p.q
                        chunk_n(2, MEM, already, lambda: transposes(xn, 0, 2))
                        transposes(xn, 2, 4)
                    else:
                        chunk_n(2, XA, already)
                        ready = normed(p.q)
                        keep_clock(18)
                        transposes(xn, 0, KD // 2)
                for c in range(p.c - 3, p.c):
                    pe.wait_ge(pair_free[c % 3], c // 3 + 1)
                pe.wait_ge(s["wrl_ready"], 1)
                for k in range(KD):
                    ready(k)
                    for n, h in enumerate((Ah, Al)):
                        ins = pe.matmul(bank(0)[0:2 * NE, 0:SEQ], wr2[:, k, :], h[:, k, :], start=k == 0 and n == 0,
                                        stop=k == KD - 1 and n == 1)
                ins.then_inc(s["logits_done"], 1)
                pe.wait_ge(s["lgT_ready"], 1)
                for t in range(NT):
                    ins = pe.matmul(bank(1)[:, t * NE:(t + 1) * NE], lgT[:, t * P:(t + 1) * P], fold[:], start=True,
                                    stop=True)
                ins.then_inc(s["lg_done"], 1)
                keep_clock(11)
                pe.wait_ge(s["hot_ready"], 1)
                sel = rt[4]
                both = sel[:].rearrange("p t e -> p (t e)")
                pe.matmul(bank(0)[:, 0:2 * NE], tri[:], both, start=True, stop=False, skip_group_check=True)
                pe.matmul(bank(0)[:, NE:2 * NE], ones[:], sel[:, 0, :], start=False, stop=True, skip_group_check=True
                          ).then_inc(s["rank_done"], 1)
                pe.matmul(bank(1)[:, 0:2 * NE], ones[:], both, start=True, stop=True).then_inc(s["count_done"], 1)

                def gather(n):
                    pe.wait_ge(s["s_ready"], n)
                    for k in range(KD):
                        o = bank(2 + k // 4)[:, (k % 4) * P:(k % 4 + 1) * P]
                        for t in range(NT):
                            ins = pe.matmul(o, hg[:, t, k * P:(k + 1) * P], S[:, t, :], start=t == 0, stop=t == NT - 1)
                        if k % 4 == 3:
                            ins.then_inc(s["g_done"], 1)

                def gate_up(j, first, o, v):
                    for part in range(2):
                        if j == 0 and first == 0:
                            pe.wait_ge(s["he_ready"], 2 * v + (part + 1))
                        u = U0 + gu_start(j) + first + part
                        pe.wait_ge(s["lo_ready"], v * BODY + (u + 1))
                        w = [t[u % SPL][:, :].rearrange("p (k n) -> p k n", k=4) for t in (whi, wlo)]
                        for k in range(4):
                            for n, (wi, xi) in enumerate(PASSES):
                                ins = pe.matmul(o, (heh, hel)[xi][:, 4 * part + k, :], w[wi][:, k, :],
                                                start=part == 0 and k == 0 and n == 0,
                                                stop=part == 1 and k == 3 and n == 2)
                        ins.then_inc(s["unit_used"], 1)

                def act_t_(j, v):
                    pe.wait_ge(s["act_ready"], v * NJ + (j + 1))
                    if j == 0:
                        pe.wait_ge(s["xadd_done"], v * 4 + 1)
                    for f in range(4):
                        ins = pe.transpose(bank(6)[:, f * P:(f + 1) * P], act_t[:, f * P:(f + 1) * P], ident[:])
                    ins.then_inc(s["t_done"], 1)

                def down(j, i0, v):
                    pe.wait_ge(s["actT_ready"], v * NJ + (j + 1))
                    for part in range(2):
                        u = U0 + i0 + part
                        pe.wait_ge(s["lo_ready"], v * BODY + (u + 1))
                        w = [t[u % SPL][:, :].rearrange("p (k n) -> p k n", k=2) for t in (whi, wlo)]
                        for k in range(2):
                            f = 2 * part + k
                            for c in range(2):
                                for n, (wi, xi) in enumerate(PASSES):
                                    ins = pe.matmul(bank(4 + c), (aTh, aTl)[xi][j % 2][:, f, :],
                                                    w[wi][:, k, c * C:(c + 1) * C],
                                                    start=j == 0 and f == 0 and n == 0,
                                                    stop=j == NJ - 1 and f == 3 and n == 2)
                        ins.then_inc(s["unit_used"], 1)

                def scatter(n, v):
                    t, c = n // 2, n % 2
                    for m, y in enumerate((yh, yl)):
                        ins = pe.matmul(bank(6 if n == 0 else 7), ST[:, t * P:(t + 1) * P], y[:, c * C:(c + 1) * C],
                                        start=m == 0, stop=m == 1)
                    ins.then_inc(s["sc_done"], 1)

                keep_clock(4)
                pe.wait_ge(s["hg_ready"], NT)
                gather(1)
                pe.wait_ge(s["zero_done"], 1)
                pe.wait_ge(s["visits_ready"], 1)
                visits = pe.value_load(nvis[0:1, 0:1], min_val=NE, max_val=2 * NE)
                with pe.Fori(0, visits) as v:
                    for j in range(NJ):
                        gate_up(j, 0, bank(2 * (j % 2)), v)
                        if j:
                            act_t_(j - 1, v)
                        gate_up(j, 2, bank(2 * (j % 2) + 1), v)
                        if j == 0:
                            pe.wait_ge(s["y_ready"], v + 1)
                            scatter(0, v)
                            scatter(1, v)
                        elif j < 3:
                            pe.wait_ge(s["xadd_done"], v * 4 + (j + 1))
                            scatter(j + 1, v)
                        elif j == 3:
                            pe.wait_ge(s["xadd_done"], v * 4 + 4)
                            pe.wait_ge(s["gate2_ready"], 1)
                            for t in range(NT):
                                pe.transpose(bank(7)[:, t * P:(t + 1) * P], S[:, t, :], ident[:])
                            for t in range(NT):
                                ins = pe.matmul(bank(7)[:, SEQ:SEQ + 1], S[:, t, :],
                                                gate2[:, t, bass.ds(v, 1)], start=t == 0, stop=t == NT - 1)
                            ins.then_inc(s["ts_done"], 1)
                        if j:
                            down(j - 1, gu_start(j) + 4, v)
                    act_t_(NJ - 1, v)
                    gather(v + 2)
                    down(NJ - 1, BODY - 2, v)

        PIECES = [(c, t) for t in range(NT) for c in range(2)]
        with nc.Block() as block:
            @block.scalar
            def _(act):
                for c in range(2):
                    act.activation(yh[:, c * C:(c + 1) * C], ps[:, 4 + c, :], ACT.Copy, scale=gc[:, 0:1]
                                   ).then_inc(s["tail_y"], 1)
                for n, (c, t) in enumerate(PIECES):
                    act.wait_ge(s["tail_x"], n + 1)
                    act.activation(xn[:, t, c * C:(c + 1) * C], x[:, t, c * C:(c + 1) * C], ACT.Square,
                                   accum_out=ss[:, 8, c, t:t + 1]).then_inc(s["tail_ss"], 1)
                act.wait_ge(s["tail_r"], 2 * 3)
                act.wait_ge(s["tail_xg"], 1)
                act.activation(hg[:, 1, :], hg[:, 1, :], ACT.Copy, scale=rstd[:, 8, 1:2]).then_inc(s["tail_o1"], 1)

            @block.vector
            def _(dve):
                for c in range(2):
                    dve.wait_ge(s["tail_y"], c + 1)
                    dve.scalar_tensor_tensor(out=yl[:, c * C:(c + 1) * C], in0=ps[:, 4 + c, :], scalar=gc[:, 0:1],
                                             in1=yh[:, c * C:(c + 1) * C].bitcast(F32), op0=ALU.mult, op1=ALU.subtract
                                             ).then_inc(s["tail_yl"], 1)
                for n, (c, t) in enumerate(PIECES):
                    dve.wait_ge(s["tail_sc"], n + 1)
                    xs = x[:, t, c * C:(c + 1) * C]
                    dve.tensor_tensor(xs, xs, bank(n), ALU.add).then_inc(s["tail_x"], 1)
                dve.wait_ge(s["gfin_loaded"], 16)
                dve.wait_ge(s["tail_r"], 3)
                dve.wait_ge(s["tail_x"], len(PIECES))
                dve.scalar_tensor_tensor(out=hg[:, 0, :], in0=x[:, 0, :], scalar=rstd[:, 8, 0:1], in1=gbc[:],
                                         op0=ALU.mult, op1=ALU.mult).then_inc(s["tail_o"], 1)
                dve.tensor_tensor(hg[:, 1, :], x[:, 1, :], gbc[:], ALU.mult).then_inc(s["tail_xg"], 1)

            @block.gpsimd
            def _(pool):
                for t in range(NT):
                    one = slice(t, t + 1)
                    pool.wait_ge(s["tail_ss"], 2 * t + 2)
                    pool.tensor_tensor(sst[:, 8, 0, one], ss[:, 8, 0, one], ss[:, 8, 1, one], ALU.add
                                       ).then_inc(s["tail_r"], 1)
                    pool.wait_ge(s["tail_r"], 3 * t + 1)
                    pool.tensor_scalar(sst[:, 8, 1, one], sst[:, 8, 0, one], 1.0 / D, EPS, ALU.mult, ALU.add
                                       ).then_inc(s["tail_r"], 1)
                    pool.wait_ge(s["tail_r"], 3 * t + 2)
                    pool.tensor_tensor(rstd[:, 8, one], sst[:, 8, 1, one], mhalf[:, one], ALU.pow
                                       ).then_inc(s["tail_r"], 1)
                    pool.wait_ge(s["tail_r"], 3 * t + 3)

            @block.tensor
            def _(pe):
                for n, (c, t) in enumerate(PIECES):
                    pe.wait_ge(s["tail_yl"], c + 1)
                    for m, y in enumerate((yh, yl)):
                        ins = pe.matmul(bank(n), ST[:, t * P:(t + 1) * P], y[:, c * C:(c + 1) * C],
                                        start=m == 0, stop=m == 1)
                    ins.then_inc(s["tail_sc"], 1)

            @block.sync
            def _(sp):
                for t, done in enumerate(("tail_o", "tail_o1")):
                    sp.wait_ge(s[done], 1)
                    sp.dma_start(out[0, t * P:(t + 1) * P, :], hg[:, t, :]).then_inc(s["stored"], 16)
                sp.wait_ge(s["stored"], 16 * NT)


def kernel(**inputs):
    import numpy as _np
    import concourse.bacc as _bacc
    from concourse import mybir as _mybir
    from concourse.bass_utils import run_bass_kernel_spmd as _run

    nc = _bacc.Bacc("TRN2", target_bir_lowering=False, num_devices=1, dynamic_dma_scratch_size=1024)
    arrays, aps = {}, {}
    for name, value in inputs.items():
        arrays[f"in_{name}"] = _np.ascontiguousarray(value)
        aps[name] = nc.dram_tensor(f"in_{name}", arrays[f"in_{name}"].shape, _mybir.dt.from_np(arrays[f"in_{name}"].dtype),
                                   kind="ExternalInput").ap()
    out = nc.dram_tensor("out_0", inputs["x"].shape, _mybir.dt.from_np(_np.dtype("float32")), kind="ExternalOutput").ap()
    trunk(nc, aps, out)
    r = _run(nc, [arrays], core_ids=[0])
    return r.results[0]["out_0"]
```
